# Optimizing a Trainium2 kernel written in Bass

```python
import math
import jax, jax.numpy as jnp
from jax import lax
import numpy as np

D_MODEL = 1024
BATCH = 1
SEQ = 512
DEPTH = 1
DEC_BATCH = 1
DEC_SEQ = 64
PAST_LEN = 256

CHUNK = 64
QBLOCK = 128
HEAD_DIM = 64
H_SPARSE = D_MODEL // 256
H_STICK = (3 * D_MODEL) // 512
H_DIFF = (3 * D_MODEL) // 512
DIFF_QK = HEAD_DIM // 2
W_SPARSE = H_SPARSE * HEAD_DIM
W_STICK = H_STICK * HEAD_DIM
W_DIFF = H_DIFF * HEAD_DIM
MIX_WIDTH = W_SPARSE + W_STICK + W_DIFF
N_IDX_HEADS = 8
IDX_DIM = 64
TOPK_MAX = 256
N_EXPERTS = 64
TOP_K = 8
D_EXPERT = D_MODEL // 8
EXPERT_GROUP = 8
ROUTED_SCALE = 2.5
RMS_EPS = 1e-6
PROJ_SIZES = (W_SPARSE, W_SPARSE, W_SPARSE, N_IDX_HEADS * IDX_DIM, IDX_DIM, N_IDX_HEADS,
              W_STICK, W_STICK, W_STICK, W_DIFF, W_DIFF, W_DIFF)
PROJ_SPLITS = tuple(sum(PROJ_SIZES[:i + 1]) for i in range(len(PROJ_SIZES) - 1))
D_PROJ = sum(PROJ_SIZES)

kernel_name = 'hybrid_streaming_encoder_dsa_stick_diff_moe_step'

def _rmsnorm(x):
    xf = x.astype(jnp.float32)
    return (xf * lax.rsqrt(jnp.mean(xf * xf, axis=-1, keepdims=True) + RMS_EPS)).astype(x.dtype)

def _alibi_slopes(n):
    return jnp.asarray([2.0 ** (-8.0 * (i + 1) / n) for i in range(n)], dtype=jnp.float32)

def _chunk(pos):
    return pos // CHUNK

def _sweep(fn, q_args, q_pos):
    tq = q_pos.shape[0]
    if tq <= QBLOCK or tq % QBLOCK:
        return fn(*q_args, q_pos)
    nb = tq // QBLOCK

    def split(a):
        return jnp.swapaxes(a.reshape(a.shape[0], nb, QBLOCK, *a.shape[2:]), 0, 1)

    out = lax.map(lambda args: fn(*args), tuple(split(a) for a in q_args) + (q_pos.reshape(nb, QBLOCK),))
    out = jnp.swapaxes(out, 0, 1)
    return out.reshape(out.shape[0], tq, *out.shape[3:])

def _sparse_attn(q, qi, wi, q_pos, k, v, ki, k_pos, topk):
    slopes = _alibi_slopes(H_SPARSE)
    rel = jax.nn.relu(jnp.einsum('bthd,bsd->bths', qi, ki).astype(jnp.float32) * IDX_DIM ** -0.5)
    score = jnp.einsum('bth,bths->bts', wi.astype(jnp.float32), rel)
    allowed = _chunk(k_pos)[None, :] <= _chunk(q_pos)[:, None]
    score = jnp.where(allowed[None], score, -jnp.inf)
    _, sel = lax.top_k(score, topk)
    sel_pos = k_pos[sel]
    valid = _chunk(sel_pos) <= _chunk(q_pos)[None, :, None]
    gather = jax.vmap(lambda a, i: a[i])
    kg = gather(k, sel)
    vg = gather(v, sel)
    logits = jnp.einsum('bthd,btkhd->bhtk', q, kg).astype(jnp.float32) * HEAD_DIM ** -0.5
    dist = jnp.abs(q_pos[None, :, None] - sel_pos).astype(jnp.float32)
    logits = logits - slopes[None, :, None, None] * dist[:, None]
    logits = jnp.where(valid[:, None], logits, -jnp.inf)
    p = jax.nn.softmax(logits, axis=-1).astype(v.dtype)
    return jnp.einsum('bhtk,btkhd->bthd', p, vg)

def _stick_attn(q, q_pos, k, v, k_pos):
    z = jnp.einsum('bthd,bshd->bhts', q, k).astype(jnp.float32) * HEAD_DIM ** -0.5
    strict = k_pos[None, :] < q_pos[:, None]
    u = jnp.where(strict, jax.nn.log_sigmoid(-z), 0.0)
    later = lax.cumsum(u, axis=3, reverse=True) - u
    a = jnp.where(strict, jnp.exp(jax.nn.log_sigmoid(z) + later), 0.0)
    return jnp.einsum('bhts,bshd->bthd', a.astype(v.dtype), v)

def _diff_attn(q, q_pos, k, v, k_pos, lam):
    slopes = _alibi_slopes(H_DIFF)
    logits = jnp.einsum('bthnd,bshnd->bnhts', q, k).astype(jnp.float32) * DIFF_QK ** -0.5
    dist = jnp.abs(q_pos[:, None] - k_pos[None, :]).astype(jnp.float32)
    allowed = _chunk(k_pos)[None, :] <= _chunk(q_pos)[:, None]
    logits = jnp.where(allowed, logits - slopes[:, None, None] * dist, -jnp.inf)
    p = jax.nn.softmax(logits, axis=-1)
    w = p[:, 0] - lam * p[:, 1]
    return jnp.einsum('bhts,bshd->bthd', w.astype(v.dtype), v)

def _moe(h, l, w_router, b_router, w_e_gate, w_e_up, w_e_down, w_s_gate, w_s_up, w_s_down):
    shp = h.shape
    t = h.reshape(-1, shp[-1])
    s = jax.nn.sigmoid((t @ w_router[l]).astype(jnp.float32))
    _, sel = lax.top_k(s + b_router[l].astype(jnp.float32), TOP_K)
    g = jnp.take_along_axis(s, sel, axis=-1)
    g = g / jnp.sum(g, axis=-1, keepdims=True) * ROUTED_SCALE
    gates = jnp.sum(jax.nn.one_hot(sel, N_EXPERTS, dtype=jnp.float32) * g[..., None], axis=1).astype(t.dtype)
    out = (jax.nn.silu(t @ w_s_gate[l]) * (t @ w_s_up[l])) @ w_s_down[l]
    for e0 in range(0, N_EXPERTS, EXPERT_GROUP):
        es = slice(e0, e0 + EXPERT_GROUP)
        a = jnp.einsum('nd,edf->nef', t, w_e_gate[l, es])
        u = jnp.einsum('nd,edf->nef', t, w_e_up[l, es])
        hid = jax.nn.silu(a) * u * gates[:, es, None]
        out = out + jnp.einsum('nef,efd->nd', hid, w_e_down[l, es])
    return out.reshape(shp)

def _layer(x, c, past, q_pos, k_pos, l, weights):
    (w_ada, b_ada, w_in, w_out, lam_diff, subln_diff, w_router, b_router,
     w_e_gate, w_e_up, w_e_down, w_s_gate, w_s_up, w_s_down) = weights
    b, t, _ = x.shape
    mod = jnp.einsum('bd,de->be', jax.nn.silu(c), w_ada[l]) + b_ada[l]
    sh1, sc1, g1, sh2, sc2, g2 = jnp.split(mod[:, None, :], 6, axis=-1)

    h = _rmsnorm(x) * (1 + sc1) + sh1
    qa, ka, va, qi, ki, wi, qb, kb, vb, qc, kc, vc = jnp.split(h @ w_in[l], PROJ_SPLITS, axis=-1)

    def heads(a, n):
        return a.reshape(b, t, n, HEAD_DIM)

    qa, ka, va = heads(qa, H_SPARSE), heads(ka, H_SPARSE), heads(va, H_SPARSE)
    qi = qi.reshape(b, t, N_IDX_HEADS, IDX_DIM)
    wi = wi * N_IDX_HEADS ** -0.5
    qb, kb, vb = heads(qb, H_STICK), heads(kb, H_STICK), heads(vb, H_STICK)
    qc = qc.reshape(b, t, H_DIFF, 2, DIFF_QK)
    kc, vc = heads(kc, H_DIFF), heads(vc, H_DIFF)
    new_rows = (jnp.stack([ka, va], axis=2), ki, jnp.stack([kb, vb], axis=2), jnp.stack([kc, vc], axis=2))
    if past is None:
        full = new_rows
    else:
        full = tuple(jnp.concatenate([p_, n_], axis=1) for p_, n_ in zip(past, new_rows))
    kva, kia, kvb, kvc = full
    n_keys = k_pos.shape[0]
    topk = min(TOPK_MAX, n_keys // 4)

    oa = _sweep(lambda q_, qi_, wi_, pos: _sparse_attn(q_, qi_, wi_, pos, kva[:, :, 0], kva[:, :, 1], kia, k_pos, topk),
                (qa, qi, wi), q_pos)
    ob = _sweep(lambda q_, pos: _stick_attn(q_, pos, kvb[:, :, 0], kvb[:, :, 1], k_pos), (qb,), q_pos)

    lam_init = 0.8 - 0.6 * math.exp(-0.3 * l)
    lv = lam_diff[l].astype(jnp.float32)
    lam = jnp.exp(jnp.sum(lv[0] * lv[1])) - jnp.exp(jnp.sum(lv[2] * lv[3])) + lam_init
    kcf = kvc[:, :, 0].reshape(b, n_keys, H_DIFF, 2, DIFF_QK)
    oc = _sweep(lambda q_, pos: _diff_attn(q_, pos, kcf, kvc[:, :, 1], k_pos, lam), (qc,), q_pos)
    oc = _rmsnorm(oc) * subln_diff[l] * (1.0 - lam_init)

    o = jnp.concatenate([oa.reshape(b, t, W_SPARSE), ob.reshape(b, t, W_STICK), oc.reshape(b, t, W_DIFF)], axis=-1)
    x = x + g1 * (o @ w_out[l])

    h2 = _rmsnorm(x) * (1 + sc2) + sh2
    x = x + g2 * _moe(h2, l, w_router, b_router, w_e_gate, w_e_up, w_e_down, w_s_gate, w_s_up, w_s_down)
    return x, new_rows

def setup_inputs(seed: int = 0) -> dict:
    key = jax.random.key(seed)
    ks = jax.random.split(key, 23)

    def nrm(k, shape, scale=1.0):
        return jax.random.normal(k, shape, jnp.float32) * scale

    d, f, e = D_MODEL, D_EXPERT, N_EXPERTS
    return {
        'x_prompt': nrm(ks[0], (BATCH, SEQ, d)),
        'x_sample': nrm(ks[1], (DEC_BATCH, DEC_SEQ, d)),
        'cache_sparse_kv': nrm(ks[2], (DEPTH, DEC_BATCH, PAST_LEN, 2, H_SPARSE, HEAD_DIM)),
        'cache_sparse_kidx': nrm(ks[3], (DEPTH, DEC_BATCH, PAST_LEN, IDX_DIM)),
        'cache_stick_kv': nrm(ks[4], (DEPTH, DEC_BATCH, PAST_LEN, 2, H_STICK, HEAD_DIM)),
        'cache_diff_kv': nrm(ks[5], (DEPTH, DEC_BATCH, PAST_LEN, 2, H_DIFF, HEAD_DIM)),
        'c_prompt': nrm(ks[6], (BATCH, d)),
        'c_sample': nrm(ks[7], (DEC_BATCH, d)),
        'w_ada': nrm(ks[8], (DEPTH, d, 6 * d), 0.5 * d ** -0.5),
        'b_ada': nrm(ks[9], (DEPTH, 6 * d), 0.02),
        'w_in': nrm(ks[10], (DEPTH, d, D_PROJ), d ** -0.5),
        'w_out': nrm(ks[11], (DEPTH, MIX_WIDTH, d), MIX_WIDTH ** -0.5),
        'lam_diff': nrm(ks[12], (DEPTH, 4, DIFF_QK), 0.1),
        'subln_diff': 1.0 + nrm(ks[13], (DEPTH, HEAD_DIM), 0.02),
        'w_router': nrm(ks[14], (DEPTH, d, e), d ** -0.5),
        'b_router': nrm(ks[15], (DEPTH, e), 0.01),
        'w_e_gate': nrm(ks[16], (DEPTH, e, d, f), d ** -0.5),
        'w_e_up': nrm(ks[17], (DEPTH, e, d, f), d ** -0.5),
        'w_e_down': nrm(ks[18], (DEPTH, e, f, d), f ** -0.5),
        'w_s_gate': nrm(ks[19], (DEPTH, d, f), d ** -0.5),
        'w_s_up': nrm(ks[20], (DEPTH, d, f), d ** -0.5),
        'w_s_down': nrm(ks[21], (DEPTH, f, d), f ** -0.5),
        'g_final': 1.0 + nrm(ks[22], (d,), 0.02),
    }

def reference(x_prompt, x_sample, cache_sparse_kv, cache_sparse_kidx, cache_stick_kv, cache_diff_kv,
              c_prompt, c_sample, w_ada, b_ada, w_in, w_out, lam_diff, subln_diff, w_router, b_router,
              w_e_gate, w_e_up, w_e_down, w_s_gate, w_s_up, w_s_down, g_final):
    weights = (w_ada, b_ada, w_in, w_out, lam_diff, subln_diff, w_router, b_router,
               w_e_gate, w_e_up, w_e_down, w_s_gate, w_s_up, w_s_down)
    s_len = x_prompt.shape[1]
    t_len = x_sample.shape[1]
    p_len = cache_sparse_kv.shape[2]
    pos_p = jnp.arange(s_len, dtype=jnp.int32)
    q_pos_s = p_len + jnp.arange(t_len, dtype=jnp.int32)
    k_pos_s = jnp.arange(p_len + t_len, dtype=jnp.int32)

    xp, xs = x_prompt, x_sample
    rows_p, rows_s = [], []
    for l in range(DEPTH):
        xp, rp = _layer(xp, c_prompt, None, pos_p, pos_p, l, weights)
        past = (cache_sparse_kv[l], cache_sparse_kidx[l], cache_stick_kv[l], cache_diff_kv[l])
        xs, rs = _layer(xs, c_sample, past, q_pos_s, k_pos_s, l, weights)
        rows_p.append(rp)
        rows_s.append(rs)
    y_prompt = _rmsnorm(xp) * g_final
    y_sample = _rmsnorm(xs) * g_final

    def stack(rows, i):
        return jnp.stack([r[i] for r in rows], axis=0)

    return (y_prompt, y_sample,
            stack(rows_p, 0), stack(rows_p, 1), stack(rows_p, 2), stack(rows_p, 3),
            stack(rows_s, 0), stack(rows_s, 1), stack(rows_s, 2), stack(rows_s, 3))


_drawn_inputs = setup_inputs


def setup_inputs(seed=0):
    import zlib

    import numpy as np

    out = dict(_drawn_inputs(seed))
    spreads = {}
    factors = {'cache_stick_kv': 2.892, 'subln_diff': 5.39, 'g_final': 2.827}
    for name, (base, spread) in spreads.items():
        noise = np.random.default_rng([zlib.crc32(name.encode()), seed]).standard_normal(out[name].shape)
        drawn = base * np.exp(spread * noise) if base else spread * noise
        out[name] = __import__('jax').numpy.asarray(drawn.astype(out[name].dtype))
    for name, factor in factors.items():
        out[name] = (out[name] * factor).astype(out[name].dtype)
    return out
```

```python
from contextlib import ExitStack

import concourse.bass as bass
from concourse import mybir

F32 = mybir.dt.float32
F32R = mybir.dt.float32r
ALU = mybir.AluOpType
ACT = mybir.ActivationFunctionType

P = 128
D = 1024
KD = D // P
N_PROMPT, N_SAMPLE, PAST = 512, 64, 256
NT = N_PROMPT + N_SAMPLE
HALF = NT // 2
N_KEYS_S = PAST + N_SAMPLE
CHUNK = 64
HD = 64
H_A, H_B, H_C = 4, 6, 6
QK_C = HD // 2
N_IDX = 8
TOPK_PROMPT, TOPK_SAMPLE = 128, 80
N_EXPERTS = 64
TOP_K = 8
F = D // 8
GROUP = 4
N_GROUPS = N_EXPERTS // GROUP
ROUTED_SCALE = 2.5
EPS = 1e-6
LAM_INIT = 0.8 - 0.6
SLOPE_A = [2.0 ** (-8.0 * (i + 1) / H_A) for i in range(H_A)]
SLOPE_C = [2.0 ** (-8.0 * (i + 1) / H_C) for i in range(H_C)]
SCALE_A = HD ** -0.5
SCALE_C = QK_C ** -0.5
BIG_Z = 30.0
NEG = -1e30
INVALID = -3e38
CHOSEN = -3.3e38
DIST0 = 384

COL = {"qa": 0, "ka": 256, "va": 512, "qi": 768, "ki": 1280, "wi": 1344,
       "qb": 1352, "kb": 1736, "vb": 2120, "qc": 2504, "kc": 2888, "vc": 3272}
TILES = ([("ki", 0), ("wi", 0)] + [("qi", i) for i in range(4)]
         + [(n, i) for n in ("qa", "ka", "va") for i in range(2)]
         + [(n, i) for n in ("qb", "kb", "vb", "qc", "kc", "vc") for i in range(3)])
N_IN = len(TILES)
SLOT = {"ki": 0, "qi": 1, "qa": 6, "ka": 8, "qb": 10, "kb": 13, "qc": 0, "kc": 3}
ROWS = ("ki", "wi", "ka", "va", "kb", "vb", "kc", "vc")
MIX = {"a": 0, "b": 2, "c": 5}


def tokens(t):
    return (P * t, P) if t < 4 else (N_PROMPT, N_SAMPLE)


def keys(t):
    return P * (t + 1) if t < 4 else N_KEYS_S


def make_schedule():
    tile = {n: i for i, n in enumerate(TILES)}
    s = []
    ada = iter(range(4, 12))

    def project(names):
        for k in names:
            s.append(("proj", tile[k]))
            if k[0] in ROWS:
                s.append(("rows", tile[k]))

    def project_with_ada(k):
        n = next(ada, None)
        s.extend([("ada", n), ("proj", tile[k]), ("turn", n)] if n is not None else [("proj", tile[k])])
        if k[0] in ROWS:
            s.append(("rows", tile[k]))

    project(TILES[:6])
    s.append(("cache", "i", 0))
    tiles = list(TILES[6:21])
    for t in (1, 2, 3, 4):
        for h in range(N_IDX):
            s.append(("score", t, h))
        s.append(("topk", t))
        for _ in range(3 if t < 4 else 2):
            project([tiles.pop(0)])
    for k in tiles:
        project_with_ada(k)
    s.append(("cache", "a", 0))
    s += [("cache", "b", 0), ("cache", "b", 1)]

    def softmax_units(units, fill=()):
        fill = list(fill)
        n = len(units)
        for i in range(n + 3):
            m = next(ada, None) if i % 4 == 0 and units[0][0] == "a" else None
            if m is not None:
                s.append(("ada", m))
            if i < n:
                s.append(("qk",) + units[i])
                s.append(("max",) + units[i])
            if m is not None:
                s.append(("turn", m))
            if 1 <= i <= n:
                s.append(("norm",) + units[i - 1])
            if fill and i % 2 == 1:
                project([fill.pop(0)])
            if 2 <= i <= n + 1:
                s.append(("pt",) + units[i - 2])
            if i >= 3:
                s.append(("pv",) + units[i - 3])
        for k in fill:
            project([k])

    softmax_units([("a", h, t) for t in (1, 2, 3, 4, 0) for h in range(H_A)], TILES[21:27])
    s += [("cache", "c", 0), ("cache", "c", 1)]
    units = [("b", h, j) for h in range(H_B) for j in (3, 2, 1, 0)] \
        + [("s", par, j) for par in (0, 1) for j in (2, 1, 0)]
    v_tiles = list(TILES[27:])
    for i in range(len(units) + 3):
        if i < len(units):
            s.append(("z",) + units[i])

        if i % 2 and v_tiles:
            project([v_tiles.pop(0)])
        steps = []
        if 1 <= i <= len(units):
            steps.append(("sp",) + units[i - 1])
        if 2 <= i <= len(units) + 1:
            steps.append(("acc",) + units[i - 2])
        s += reversed(steps) if steps and steps[0][1] == "s" else steps
        if i >= 3:
            s.append(("av",) + units[i - 3])

    assert next(ada, None) is None
    softmax_units([("c", h, t) for h in range(H_C) for t in range(5)])
    return s


SCHEDULE = make_schedule()
STEP_AT = {step: i for i, step in enumerate(SCHEDULE)}


class Ring:

    def __init__(self, size, full, free):
        self.size, self.full, self.free = size, full, free
        self.n, self.fills, self.uses = 0, [0] * size, [0] * size
        self.at = {}

    def use(self, key, fills=1):
        b = self.n % self.size
        self.n += 1
        self.at[key] = (b, self.uses[b], self.fills[b])
        self.fills[b] += fills
        self.uses[b] += 1

    def bank(self, key):
        return self.at[key][0]

    def wait_free(self, eng, key):
        b, before, _ = self.at[key]
        if before:
            eng.wait_ge(self.free[b], before)

    def wait_full(self, eng, key, fill=1):
        b, _, fills = self.at[key]
        eng.wait_ge(self.full[b], fills + fill)

    def wait_taken(self, eng, key):
        b, before, _ = self.at[key]
        eng.wait_ge(self.free[b], before + 1)

    def fill(self, ins, key):
        ins.then_inc(self.full[self.at[key][0]], 1)

    def take(self, ins, key):
        ins.then_inc(self.free[self.at[key][0]], 1)


def build(nc, io):
    ctx = ExitStack()
    with ctx:
        def sb(name, shape, dt=F32, stack=ctx):
            return stack.enter_context(nc.sbuf_tensor(name, shape, dt))

        def sem(name):
            return ctx.enter_context(nc.semaphore(name))

        bank = [ctx.enter_context(nc.psum_tensor(f"bank{i}", [P, 512], F32)) for i in range(8)]
        x_spill = nc.dram_tensor("x_spill", (P, KD, NT), F32).ap()
        gate_rows = nc.dram_tensor("gate_rows", (N_EXPERTS, NT), F32).ap()

        resid = sb("resid", [P, KD, NT])
        h_hi = sb("h_hi", [P, KD, NT], F32R)
        h_lo = sb("h_lo", [P, KD, NT], F32R)
        ident = sb("ident", [P, P])
        ones = sb("ones", [P, P])

        vec = sb("vec", [P, 73])
        silu_c = sb("silu_c", [P, KD, 2])


        mod = sb("mod", [P, 6 * KD, 2])
        std = sb("std", [P, NT])
        rstd = sb("rstd", [P, NT])
        vec_rows = rstd[0:73, 0:P]
        mod_rows = std[0:2, 0:512]
        eps_col = sb("eps_col", [P, 1])

        early = ExitStack()
        ea = lambda name, shape, dt=F32: sb(name, shape, dt, early)
        feat2 = ea("feat2", [P, 8, NT])
        o_t = ea("o_t", [P, KD, NT])
        v_t = ea("v_t", [P, 2, NT])
        pro = ExitStack()
        x_rows = sb("x_rows", [P, 2, D], F32, pro)
        sq = sb("sq", [P, 2, NT], F32, pro)
        hf = sb("hf", [P, 2, NT], F32, pro)
        pro.close()
        v_rows = [ea(f"v_rows{i}", [P, 7, 384]) for i in range(2)]
        cache_rows = ea("cache_rows", [P, 2, 384])
        cache_t = ea("cache_t", [P, 2, 3, PAST])
        pick_stack = ExitStack()
        pick = {t: sb(f"pick{t}", [P, keys(t)], F32, pick_stack) for t in (1, 2, 3, 4)}
        pick_stack.close()
        sp_buf = ea("sp_buf", [P, 3, 512])
        w_stage = ea("w_stage", [P, 4, KD, P])
        w_hi = ea("w_hi", [P, 2, KD, P], F32R)
        w_lo = ea("w_lo", [P, 2, KD, P], F32R)
        k_rows = ea("k_rows", [P, 2, 5, P])
        wi_rows = ea("wi_rows", [P, 5, N_IDX])
        neg_tri = ea("neg_tri", [P, P])
        neg_ones = ea("neg_ones", [P, P])
        diag_neg = ea("diag_neg", [P, P])
        diag_01 = ea("diag_01", [P, P])
        diag_neg_s = ea("diag_neg_s", [N_SAMPLE, H_B // 2, N_SAMPLE])
        diag_01_s = ea("diag_01_s", [N_SAMPLE, H_B // 2, N_SAMPLE])
        two_heads = ea("two_heads", [P, P])
        dist = ea("dist", [P, 512])
        lam_rows = ea("lam_rows", [P, 4 * QK_C])
        lam_dot = ea("lam_dot", [P, 2])
        lam_exp = ea("lam_exp", [P, 2])
        lam_fac = ea("lam_fac", [P, 2])
        max8 = ea("max8", [P, 8])
        bias = ea("bias", [P, 2, 512])
        p_work = ea("p_work", [P, 6, 512])
        turned = ExitStack()
        p_t = sb("p_t", [P, 2, 4, P], F32, turned)
        turned.close()
        l_buf = ea("l_buf", [P, 2, 512])
        n_max = ea("n_max", [P, 2, 2])
        p_sum = ea("p_sum", [P, 2, 2])
        p_rec = ea("p_rec", [P, 2, 2])
        run = ea("run", [P, 2, 384])
        a_t = ea("a_t", [P, 2, 512])
        early.close()

        late = ExitStack()
        la = lambda name, shape, dt=F32: sb(name, shape, dt, late)
        y_acc = la("y_acc", [P, KD, NT])
        gu_stage = la("gu_stage", [P, 2, 2, KD, F])
        gu_hi = la("gu_hi", [P, 2, 2, KD, F], F32R)
        gu_lo = la("gu_lo", [P, 2, 2, KD, F], F32R)
        d_stage = la("d_stage", [P, GROUP, D])
        d_hi = la("d_hi", [P, 2, GROUP, P], F32R)
        d_lo = la("d_lo", [P, 2, GROUP, P], F32R)
        hid_hi = la("hid_hi", [P, GROUP, NT], F32R)
        hid_lo = la("hid_lo", [P, GROUP, NT], F32R)
        gate_bc = la("gate_bc", [P, GROUP, NT])
        sg = la("sg", [P, 2, NT])
        hidf = la("hidf", [P, 2, NT])
        r_rows = la("r_rows", [P, 5, 3, N_EXPERTS])
        r_max = la("r_max", [P, 5, 8])
        r_sum = la("r_sum", [P, 5, 2])
        gate_t = la("gate_t", [N_EXPERTS, NT])
        b_rows = la("b_rows", [P, N_EXPERTS])
        r_hi = la("r_hi", [P, KD, N_EXPERTS], F32R)
        r_lo = la("r_lo", [P, KD, N_EXPERTS], F32R)
        late.close()
        r_stage = d_stage[:, 0, 0:KD * N_EXPERTS].rearrange("p (k n) -> p k n", k=KD)

        consts = sem("consts")
        vec_in, lam_in, router_in = sem("vec_in"), sem("lam_in"), sem("router_in")
        vec_turned, vec_ready, silu_ready = sem("vec_turned"), sem("vec_ready"), sem("silu_ready")
        lam_dots, lam_exps = sem("lam_dots"), sem("lam_exps")
        x_in = [sem(f"x_in{i}") for i in range(2)]
        xt_full, xt_taken, spilled, resid_in = sem("xt_full"), sem("xt_taken"), sem("spilled"), sem("resid_in")
        sq_ready, sq_used, std_ready, rstd_ready = sem("sq_ready"), sem("sq_used"), sem("std_ready"), sem("rstd_ready")
        norm_ready, c_normed = sem("norm_ready"), sem("c_normed")
        hf_ready, h_hi_ready, h_lo_ready = sem("hf_ready"), sem("h_hi_ready"), sem("h_lo_ready")
        w_in_s = [sem(f"w_in{i}") for i in range(4)]
        w_hi_ready, w_lo_ready = sem("w_hi_ready"), sem("w_lo_ready")
        ada_rows, rows_copied, ada_full = sem("ada_rows"), sem("rows_copied"), sem("ada_full")
        proj_full, proj_taken, resid_ready = sem("proj_full"), sem("proj_taken"), sem("resid_ready")
        qk_full = [sem(f"qk_full{i}") for i in range(3)]
        qk_free = [sem(f"qk_free{i}") for i in range(3)]
        tr_full = [sem(f"tr_full{i}") for i in range(2)]
        tr_free = [sem(f"tr_free{i}") for i in range(2)]
        o_full, o_free = sem("o_full"), sem("o_free")
        cache_in, v_cache_in = sem("cache_in"), sem("v_cache_in")
        k_rows_out = [sem(f"k_rows_out{i}") for i in range(2)]
        rows_out = sem("rows_out")
        score_ready, picked = sem("score_ready"), sem("picked")
        bias_ready, exp_ready, p_ready = sem("bias_ready"), sem("exp_ready"), sem("p_ready")
        l_ready, capped, sp_ready, run_ready = sem("l_ready"), sem("capped"), sem("sp_ready"), sem("run_ready")
        av_done = sem("av_done")
        dve_step, act_step = sem("dve_step"), sem("act_step")
        r_full, r_taken, gates_ready, gates_turned, gates_copied, gates_out = (
            sem("r_full"), sem("r_taken"), sem("gates_ready"), sem("gates_turned"), sem("gates_copied"), sem("gates_out"))
        gu_in = [sem(f"gu_in{i}") for i in range(2)]
        d_in = sem("d_in")
        g_in = [sem(f"g_in{i}") for i in range(GROUP)]
        gu_hi_ready, gu_lo_ready, d_hi_ready, d_lo_ready = (
            sem("gu_hi_ready"), sem("gu_lo_ready"), sem("d_hi_ready"), sem("d_lo_ready"))
        au_full, sg_ready, gated, hid_ready = sem("au_full"), sem("sg_ready"), sem("gated"), sem("hid_ready")
        hid_hi_ready, hid_lo_ready, down_full, y_added = (
            sem("hid_hi_ready"), sem("hid_lo_ready"), sem("down_full"), sem("y_added"))
        fin_ready, y_full, y_taken = sem("fin_ready"), sem("y_full"), sem("y_taken")
        y_out = [sem(f"y_out{i}") for i in range(2)]

        qk = Ring(3, qk_full, qk_free)
        tr = Ring(2, tr_full, tr_free)
        o_uses, n_o = {}, 0
        for n in range(4):
            tr.use(("ada", n), fills=0)
        for step in SCHEDULE:
            kind = step[0]
            if kind == "score":
                qk.use(step)
            elif kind == "qk":
                for m in range(2 if step[1] == "c" else 1):
                    qk.use(step[1:] + (m,))
            elif kind == "z":
                qk.use(step[1:], fills=2)
            elif kind == "rows":
                tr.use(step + (0,))
                tr.use(step + (1,))
            elif kind in ("pt", "cache"):
                tr.use(step)
            elif kind == "ada":
                tr.use(step, fills=0)
            if kind == "pv" or (kind == "av" and step[3] == 0):
                o_uses[step] = n_o
                n_o += 1
        score_bank, tr_bank, o_bank = bank[2:5], bank[5:7], bank[7]

        proj_no = {step[1]: i for i, step in enumerate(x for x in SCHEDULE if x[0] == "proj")}
        assert all(proj_no[i] == i for i in range(N_IN))
        N_SPLIT = N_IN + KD
        stage_order = [("ada", n) for n in range(16)] + [("w", 0)]
        for step in SCHEDULE:
            if step[0] == "ada":
                stage_order += [("ada", 4 * step[1] + i) for i in range(4)]
            if step[0] == "proj":
                stage_order.append(("w", step[1] + 1))
        stage_order += [("w", N_IN + i) for i in range(1, KD)]
        stage_no = {item: i for i, item in enumerate(stage_order)}
        stage_value, _v = {}, [0] * 4
        for i, item in enumerate(stage_order):
            _v[i % 4] += 32 if item == ("w", 0) else 16
            stage_value[item] = _v[i % 4]

        def wait_stage(eng, item):
            eng.wait_ge(w_in_s[stage_no[item] % 4], stage_value[item])

        def staged(item):
            return w_stage[:, stage_no[item] % 4]

        def index_of(kinds):
            return {st: i for i, st in enumerate(x for x in SCHEDULE if x[0] in kinds)}

        score_no = index_of(("score",))
        unit_no = {st[1:]: i for st, i in index_of(("qk",)).items()}
        stick_no = {st[1:]: i for st, i in index_of(("z",)).items()}
        unit_key = {i: k for k, i in unit_no.items()}
        stick_key = {i: k for k, i in stick_no.items()}
        rows_steps = [x for x in SCHEDULE if x[0] == "rows"]
        k_fill = {}
        for st in rows_steps:
            if TILES[st[1]][0][0] == "k":
                k_fill[st] = len(k_fill)
        map_no, n_maps = {}, 0
        for st in SCHEDULE:
            if st[0] == "qk":
                for m in range(2 if st[1] == "c" else 1):
                    map_no[st[1:] + (m,)] = n_maps
                    n_maps += 1

        def feat(slot):
            return resid[:, slot, :] if slot < 8 else feat2[:, slot - 8, :]

        def v_of(group):
            return v_rows[1 if group in ("b", "s") else 0]

        def cache_slot(group):
            return {"i": 0, "a": 1, "b": 0, "c": 1}[group]

        def last_step(pred):
            return [x for x in SCHEDULE if pred(x)][-1]

        last_score = last_step(lambda x: x[0] == "score")
        last_a_pv = last_step(lambda x: x[0] == "pv" and x[1] == "a")
        last_c_pv = last_step(lambda x: x[0] == "pv" and x[1] == "c")
        last_a_qk = last_step(lambda x: x[0] == "qk" and x[1] == "a")

        def cache_blocks(g, part):
            nf = {"i": 1, "a": 2, "b": 3, "c": 3}[g]
            return [(f, t) for f in range(nf) for t in range(2)][4 * part:4 * part + 4]

        def stick_rows(key):
            return N_SAMPLE if key[0] == "s" and key[2] == 2 else P

        def stick_width(key):
            return H_B // 2 * N_SAMPLE if key[0] == "s" else N_PROMPT - P * key[2]

        row_sources = [st[1] for st in rows_steps if TILES[st[1]][0][0] in "vw"]
        sq_base = [0, KD + 3, 2 * KD + 3]

        def split_low(eng, e, n):
            eng.wait_ge(w_hi_ready, n + 1)
            e.tensor_tensor(w_lo[:, n % 2], staged(("w", n)), w_hi[:, n % 2].bitcast(F32), ALU.subtract)\
                .then_inc(w_lo_ready, 1)

        def vector_splits(step):
            return STEP_AT[("topk", 4)] < STEP_AT[step] < STEP_AT[("qk", "a", 0, 1)]

        def y_acc_rows(t):
            return gu_stage[:, t % 2, 0].rearrange("p k f -> p (k f)")

        def constants(pool, first):
            g = nc.gpsimd
            n = 0 if first else 2

            def made(ins):
                nonlocal n
                n += 1
                ins.then_inc(consts, 1)
                pool.wait_ge(consts, n)

            def masked(t, fill0, pattern, cm, op, fill):
                made(g.memset(t, fill0))
                made(g.affine_select(out=t, in_=t, compare_op=op, fill=fill, base=0, pattern=pattern,
                                     channel_multiplier=cm))

            if first:
                masked(ident[:, :], 0.0, [[-1, P]], 1, ALU.not_equal, 1.0)
                return
            made(g.memset(eps_col[:, :], EPS))
            made(g.memset(ones[:, :], 1.0))
            made(g.memset(neg_ones[:, :], -1.0))
            masked(neg_tri[:, :], -1.0, [[-1, P]], 1, ALU.is_ge, 0.0)
            masked(diag_neg[:, :], 0.0, [[1, P]], -1, ALU.is_gt, NEG)
            masked(diag_01[:, :], 1.0, [[1, P]], -1, ALU.is_gt, 0.0)
            masked(diag_neg_s[:, :, :], 0.0, [[0, H_B // 2], [1, N_SAMPLE]], -1, ALU.is_gt, NEG)
            masked(diag_01_s[:, :, :], 1.0, [[0, H_B // 2], [1, N_SAMPLE]], -1, ALU.is_gt, 0.0)
            made(g.memset(two_heads[:, :], 0.0))
            made(g.memset(two_heads[0:HD, 0:HD], 1.0))
            made(g.memset(two_heads[HD:P, HD:P], 1.0))
            made(g.iota(dist[:, :], pattern=[[-1, 512]], base=DIST0, channel_multiplier=1,
                        allow_small_or_imprecise_dtypes=True))

        N_CONSTS = 6 * 2 + 2 + 3 + 2

        block = ctx.enter_context(nc.Block())

        @block.sync
        def _(sp):
            w_ada = io["w_ada"][0].rearrange("(k p) e -> p k e", p=P)
            w_in = io["w_in"][0].rearrange("(k p) e -> p k e", p=P)
            w_out = io["w_out"][0].rearrange("(k p) e -> p k e", p=P)
            for i, item in enumerate(stage_order):
                if i >= 4:
                    before, n_before = stage_order[i - 4]
                    sp.wait_ge(w_lo_ready if before == "w" else ada_rows, n_before + 1)
                dst = w_stage[:, i % 4]
                s = w_in_s[i % 4]
                kind, n = item
                if kind == "ada":
                    sp.dma_start(dst, w_ada[:, :, P * n:P * n + P]).then_inc(s, 16)
                elif n >= N_IN:
                    e = n - N_IN
                    sp.dma_start(dst, w_out[:, :, P * e:P * e + P]).then_inc(s, 16)
                elif n == 0:
                    c = COL["ki"]
                    for j in range(2):
                        sp.dma_start(dst[:, :, HD * j:HD * j + HD], w_in[:, :, c:c + HD]).then_inc(s, 16)
                else:
                    name, j = TILES[n]
                    c = COL[name] + P * j
                    sp.dma_start(dst, w_in[:, :, c:c + P]).then_inc(s, 16)

            gate_up = [io["w_e_gate"][0].rearrange("e (k p) f -> e p k f", p=P),
                       io["w_e_up"][0].rearrange("e (k p) f -> e p k f", p=P)]
            down = io["w_e_down"][0].rearrange("(g e) f d -> g f e d", e=GROUP)
            sp.wait_ge(resid_ready, 2 * KD)
            sp.dma_start(r_stage, io["w_router"][0].rearrange("(k p) n -> p k n", p=P)).then_inc(router_in, 16)
            sp.dma_start(b_rows[:, :], io["b_router"].broadcast_to([P, N_EXPERTS])).then_inc(router_in, 16)
            for m, name in enumerate(("w_s_gate", "w_s_up")):
                sp.dma_start(gu_stage[:, 0, m], io[name][0].rearrange("(k p) f -> p k f", p=P)).then_inc(gu_in[0], 16)

            def load_gate_up(g, e):
                if isinstance(g, int) and g == 0 and e == 0:
                    pass
                else:
                    sp.wait_ge(gu_lo_ready, g * GROUP + e)
                for m in range(2):
                    sp.dma_start(gu_stage[:, (1 + e) % 2, m], gate_up[m][g * GROUP + e])\
                      .then_inc(gu_in[(1 + e) % 2], 16)

            def load_down(g):
                sp.wait_ge(d_lo_ready, g * KD + KD)
                sp.dma_start(d_stage[:, :, :], down[g]).then_inc(d_in, 16)

            load_gate_up(0, 0)
            sp.wait_ge(r_taken, 2)
            sp.dma_start(d_stage[:, 0, :], io["w_s_down"][0]).then_inc(d_in, 16)
            load_gate_up(0, 1)
            load_down(0)
            load_gate_up(0, 2)
            load_gate_up(0, 3)
            with sp.Fori(1, N_GROUPS) as g:
                load_gate_up(g, 0)
                load_gate_up(g, 1)
                load_down(g)
                load_gate_up(g, 2)
                load_gate_up(g, 3)

            y_p = io["y_prompt"].rearrange("b (t p) d -> (b t) p d", p=P)
            for t in range(5):
                sp.wait_ge(y_taken, 2 * t + 2)
                n = tokens(t)[1]
                dst = y_p[t] if t < 4 else io["y_sample"][0]
                sp.dma_start(dst, y_acc_rows(t)[0:n, :]).then_inc(y_out[t % 2], 16)
            sp.wait_ge(y_out[0], 48)
            sp.wait_ge(y_out[1], 32)

        @block.gpsimd
        def _(pool):
            for name, r0, n in (("b_ada", 0, 48), ("g_final", 48, 8), ("c_prompt", 56, 8), ("c_sample", 64, 8)):
                a = io[name] if name == "g_final" else io[name][0]
                pool.dma_start(vec_rows[r0:r0 + n, :], a.rearrange("(r c) -> r c", c=P)).then_inc(vec_in, 16)
            for j in range(2):
                pool.dma_start(vec_rows[72:73, HD * j:HD * j + HD], io["subln_diff"]).then_inc(vec_in, 16)
            xp = io["x_prompt"].rearrange("b (t p) d -> (b t) p d", p=P)
            for t in range(5):
                if t >= 2:
                    pool.wait_ge(xt_taken, 2 * (t - 1))
                n = tokens(t)[1]
                pool.dma_start(x_rows[0:n, t % 2, :], xp[t] if t < 4 else io["x_sample"][0]).then_inc(x_in[t % 2], 16)
                if t == 1:
                    constants(pool, True)
            constants(pool, False)
            pool.dma_start(lam_rows[:, :], io["lam_diff"].rearrange("l a b -> l (a b)").broadcast_to([P, 4 * QK_C]))\
                .then_inc(lam_in, 16)
            pool.wait_ge(xt_taken, 10)
            pool.dma_start(x_spill, o_t[:, :, :]).then_inc(spilled, 16)

            caches = {"i": io["cache_sparse_kidx"][0, 0], "a": io["cache_sparse_kv"][0, 0],
                      "b": io["cache_stick_kv"][0, 0], "c": io["cache_diff_kv"][0, 0]}
            width = {"a": H_A * HD, "b": H_B * HD, "c": H_C * HD}

            def load_cache(g):
                if g == "i":
                    src = caches[g].rearrange("(t p) c -> p t c", p=P)
                    for j in range(2):
                        pool.dma_start(cache_rows[:, :, HD * j:HD * j + HD], src).then_inc(cache_in, 16)
                    return
                src = caches[g].rearrange("(t p) kv h d -> p t kv (h d)", p=P)
                before = {"a": ("cache", "i", 0), "b": ("cache", "a", 0), "c": ("cache", "b", 1)}[g]
                tr.wait_full(pool, before)
                pool.dma_start(cache_rows[:, :, 0:width[g]], src[:, :, 0, :]).then_inc(cache_in, 16)
                if g == "c":
                    pool.wait_ge(o_full, unit_no[last_a_pv[1:]] + 1)
                pool.dma_start(v_of(g)[:, 4:6, 0:width[g]], src[:, :, 1, :]).then_inc(v_cache_in, 16)

            out_p = {"ki": io["ki_p"], "ka": io["kv_a_p"][:, 0], "va": io["kv_a_p"][:, 1],
                     "kb": io["kv_b_p"][:, 0], "vb": io["kv_b_p"][:, 1],
                     "kc": io["kv_c_p"][:, 0], "vc": io["kv_c_p"][:, 1]}
            out_s = {"ki": io["ki_s"], "ka": io["kv_a_s"][:, 0], "va": io["kv_a_s"][:, 1],
                     "kb": io["kv_b_s"][:, 0], "vb": io["kv_b_s"][:, 1],
                     "kc": io["kv_c_s"][:, 0], "vc": io["kv_c_s"][:, 1]}

            def store_rows(step):
                name, j = TILES[step[1]]
                if name == "wi":
                    return
                w = HD if name == "ki" else P
                for half in range(2):
                    tr.wait_taken(pool, step + (half,))
                if name[0] == "k":
                    n = k_fill[step]
                    src_p, src_s = k_rows[:, n % 2, 0:4, 0:w], k_rows[0:N_SAMPLE, n % 2, 4, 0:w]
                    s = k_rows_out[n % 2]
                else:
                    v = v_of(name[1])
                    src_p, src_s = v[:, 0:4, P * j:P * j + w], v[0:N_SAMPLE, 6, P * j:P * j + w]
                    s = rows_out
                pool.dma_start(out_p[name].rearrange("(t p) c -> p t c", p=P)[:, :, P * j:P * j + w], src_p)\
                    .then_inc(s, 16)
                pool.dma_start(out_s[name][:, P * j:P * j + w], src_s).then_inc(s, 16)

            load_cache("i")
            for step in SCHEDULE:
                if step[0] == "proj" and not vector_splits(step):
                    pool.wait_ge(w_lo_ready, step[1] + 1)
                    split_low(pool, nc.gpsimd, step[1] + 1)
                if step[0] == "rows":
                    store_rows(step)
                if step == ("score", 1, 0):
                    load_cache("a")
                if step == ("cache", "a", 0):
                    load_cache("b")
                if step == ("cache", "c", 0):
                    load_cache("c")
                if step[0] == "max" and step[1] == "c" and step[3] == 0:
                    h = step[2]
                    if h >= 2:
                        for t in range(5):
                            qk.wait_taken(pool, ("c", h - 2, t, 1))
                    elif h == 0:
                        for u in range(H_A):
                            qk.wait_taken(pool, ("a", u, 0, 0))
                    nc.gpsimd.tensor_scalar(bias[:, h % 2, :], dist[:, :], -SLOPE_C[h] / SCALE_C, None, ALU.mult)\
                        .then_inc(bias_ready, 1)
            for m in range(2):
                qk.wait_full(pool, ("c", H_C - 1, 4, m))
            pool.wait_ge(spilled, 16)
            pool.dma_start(resid[:, :, :], x_spill).then_inc(resid_in, 16)
            for i in range(2):
                pool.wait_ge(k_rows_out[i], 32 * len([n for n in k_fill.values() if n % 2 == i]))
            pool.wait_ge(rows_out, 32 * 8)

            pool.wait_ge(gated, 2 * GROUP)
            pool.dma_start(gate_rows, gate_t[:, :]).then_inc(gates_out, 16)
            pool.wait_ge(gates_out, 16)
            with pool.Fori(0, N_GROUPS) as g:
                for e in range(GROUP):
                    pool.wait_ge(gated, (g * GROUP + e + 1) * 2)
                    pool.dma_start(gate_bc[:, e, :], gate_rows[bass.ds(g * GROUP + e, 1), :].broadcast_to([P, NT]))\
                        .then_inc(g_in[e], 16)

        @block.scalar
        def _(act):
            n_step = 0

            def chain(ins):
                nonlocal n_step
                n_step += 1
                ins.then_inc(act_step, 1)
                act.wait_ge(act_step, n_step)

            def squares(r, src):
                for k in range(KD):
                    m = KD * r + k
                    if k >= 2:
                        act.wait_ge(sq_used, m - 1)
                    nc.scalar.activation(sq[:, k % 2, :], src(k), ACT.Square).then_inc(sq_ready, 1)
                act.wait_ge(sq_used, KD * (r + 1))
                for b in range(2):
                    nc.scalar.activation(std[:, HALF * b:HALF * b + HALF], bank[b][:, 0:HALF], ACT.Sqrt,
                                         scale=1.0 / D, bias=eps_col[:, 0:1]).then_inc(std_ready, 1)

            def split_high(n):
                wait_stage(act, ("w", n))
                if n >= 2:
                    act.wait_ge(proj_full, 2 * (n - 1))
                nc.scalar.copy(w_hi[:, n % 2], staged(("w", n))).then_inc(w_hi_ready, 1)

            def modulated(dst, c, normed, affine):
                for k in range(KD):
                    w = dst[:, k % 2, :]
                    act.wait_ge(norm_ready, normed + k + 1)
                    for b, (a, z) in enumerate(((0, N_PROMPT), (N_PROMPT, NT))):
                        nc.scalar.activation(w[:, a:z], w[:, a:z], ACT.Identity, scale=mod[:, c + KD + k, b:b + 1],
                                             bias=mod[:, c + k, b:b + 1]).then_inc(hf_ready, 1)
                    act.wait_ge(hf_ready, affine + 2 * k + 2)
                    nc.scalar.copy(h_hi[:, k, :], w).then_inc(h_hi_ready, 1)

            act.wait_ge(vec_ready, 1)
            nc.scalar.activation(silu_c[:, :, :].rearrange("p k b -> p b k"),
                                 vec[:, 56:72].rearrange("p (b k) -> p b k", b=2), ACT.Silu).then_inc(silu_ready, 1)

            act.wait_ge(xt_taken, 10)
            act.wait_ge(ada_full, 4)
            act.wait_ge(consts, N_CONSTS)
            split_high(0)
            squares(0, lambda k: o_t[:, k, :])
            act.preload_act_table_set("natural_log_exp_and_others")
            modulated(hf, 0, 0, 0)
            act.wait_ge(lam_dots, 2)
            nc.scalar.activation(lam_exp[:, :], lam_dot[:, :], ACT.Exp).then_inc(lam_exps, 1)

            def evacuate_projection(n):
                name, j = TILES[n]
                for b in range(2):
                    act.wait_ge(proj_full, 2 * n + b + 1)
                    if name in ("wi", "va", "vb", "vc"):
                        m = row_sources.index(n)
                        dst = v_t[:, m % 2, :]
                        if b == 0 and m >= 2:
                            for half in range(2):
                                tr.wait_full(act, ("rows", row_sources[m - 2], half))
                    else:
                        dst = feat(SLOT[name] + j)
                        if b == 0 and name in ("qc", "kc"):
                            qk.wait_full(act, last_score)
                    nc.scalar.activation(dst[:, HALF * b:HALF * b + HALF], bank[b][:, 0:HALF], ACT.Copy,
                                         scale=SCALE_A if name == "qb" else 1.0).then_inc(proj_taken, 1)

            def evacuate_rows(step):
                name, j = TILES[step[1]]
                key = [step + (i,) for i in range(2)]
                src = [tr_bank[tr.bank(k)] for k in key]
                if name == "wi":
                    w, scale = N_IDX, N_IDX ** -0.5
                    dst = [wi_rows[:, 0:4, :], wi_rows[0:N_SAMPLE, 4, :]]
                elif name[0] == "k":
                    w, scale = HD if name == "ki" else P, 1.0
                    n = k_fill[step]
                    if n >= 2:
                        act.wait_ge(k_rows_out[n % 2], 32 * (n // 2))
                    dst = [k_rows[:, n % 2, 0:4, 0:w], k_rows[0:N_SAMPLE, n % 2, 4, 0:w]]
                else:
                    w, scale = P, 1.0
                    v = v_of(name[1])
                    if name == "vc" and j == 0:
                        act.wait_ge(o_full, unit_no[last_a_pv[1:]] + 1)
                        act.wait_ge(rows_out, 32 * 5)
                    dst = [v[:, 0:4, P * j:P * j + P], v[0:N_SAMPLE, 6, P * j:P * j + P]]
                tr.wait_full(act, key[0])
                nc.scalar.activation(dst[0], src[0][:, 0:4 * w].rearrange("p (t c) -> p t c", t=4), ACT.Copy,
                                     scale=scale).then_inc(tr_free[tr.bank(key[0])], 1)
                tr.wait_full(act, key[1])
                nc.scalar.activation(dst[1], src[1][0:N_SAMPLE, 0:w], ACT.Copy, scale=scale)\
                    .then_inc(tr_free[tr.bank(key[1])], 1)

            for step in SCHEDULE:
                kind, key = step[0], step[1:]
                if kind == "proj":
                    split_high(step[1] + 1)
                    evacuate_projection(step[1])
                elif kind == "rows":
                    evacuate_rows(step)
                elif kind == "cache":
                    g, part = key
                    tr.wait_full(act, step)
                    blocks = cache_blocks(g, part)
                    f0 = blocks[0][0]
                    nf = len(blocks) // 2
                    if part == 0 and g == "b":
                        qk.wait_full(act, last_score)
                    if part == 0 and g == "c":
                        qk.wait_full(act, last_a_qk[1:] + (0,))
                    nc.scalar.copy(cache_t[:, cache_slot(g), f0:f0 + nf, :],
                                   tr_bank[tr.bank(step)][:, 0:256 * nf].rearrange("p (f c) -> p f c", f=nf))\
                        .then_inc(tr_free[tr.bank(step)], 1)
                elif kind == "score":
                    t, h = key
                    n, m = keys(t), score_no[step]
                    rows = tokens(t)[1]
                    qk.wait_full(act, step)
                    if m >= 2:
                        act.wait_ge(score_ready, m - 1)
                    qk.take(nc.scalar.activation(bias[0:rows, m % 2, 0:n], score_bank[qk.bank(step)][0:rows, 0:n],
                                                 ACT.Relu, scale=HD ** -0.5), step)
                elif kind == "max":
                    g, h, t = key
                    rows, n, u = tokens(t)[1], keys(t), unit_no[key]
                    for m in range(2 if g == "c" else 1):
                        qk.wait_taken(act, key + (m,))
                        w = p_work[0:rows, 2 * (u % 3) + m, 0:n]
                        nc.scalar.activation(w, w, ACT.Exp, scale=-1.0, bias=n_max[0:rows, u % 2, m:m + 1],
                                             accum_out=p_sum[0:rows, u % 2, m:m + 1]).then_inc(exp_ready, 1)
                elif kind == "pt":
                    g, h, t = key
                    rows, n, u = tokens(t)[1], keys(t), unit_no[key]
                    tr.wait_full(act, step)
                    if u >= 2:
                        act.wait_ge(o_full, u - 1)
                    if key == ("c", 0, 0):
                        act.wait_ge(sp_ready, len(stick_no))
                    src = tr_bank[tr.bank(step)]
                    full = n // P
                    ins = nc.scalar.copy(p_t[:, u % 2, 0:full, 0:rows],
                                         src[:, 0:full * rows].rearrange("p (j q) -> p j q", j=full))
                    if n % P:
                        chain(ins)
                        ins = nc.scalar.copy(p_t[0:n % P, u % 2, full, 0:rows],
                                             src[0:n % P, full * rows:(full + 1) * rows])
                    ins.then_inc(tr_free[tr.bank(step)], 1)
                elif kind == "z":
                    rows, w, u = stick_rows(key), stick_width(key), stick_no[key]
                    act.wait_ge(capped, u + 1)
                    l = l_buf[0:rows, u % 2, 0:w]
                    chain(nc.scalar.activation(l, l, ACT.Exp))
                    nc.scalar.activation(l, l, ACT.Ln, bias=1.0).then_inc(l_ready, 1)
                elif kind == "acc":
                    rows, w, u = stick_rows(key), stick_width(key), stick_no[key]
                    qk.wait_full(act, key, 2)
                    if u >= 2:
                        act.wait_ge(av_done, u - 1)
                    b = qk.bank(key)
                    qk.take(nc.scalar.activation(a_t[0:rows, u % 2, 0:w], score_bank[b][0:rows, 0:w], ACT.Exp), key)

            act.wait_ge(ada_full, 12)
            for i in range(3):
                act.wait_ge(o_free, n_o)
                act.wait_ge(rows_out, 32 * 8)
                nc.scalar.activation(sq[:, i % 2, :], o_t[:, MIX["c"] + i, :], ACT.Square).then_inc(sq_ready, 1)
                act.wait_ge(sq_used, KD + i + 1)
                act.wait_ge(rstd_ready, 1 + i)
                for b in range(2):
                    nc.scalar.activation(std[:, HALF * b:HALF * b + HALF], score_bank[b][:, 0:HALF], ACT.Sqrt,
                                         scale=1.0 / HD, bias=eps_col[:, 0:1]).then_inc(std_ready, 1)
            for k in range(KD):
                if k == 0:
                    act.wait_ge(proj_full, 2 * N_IN)
                if k >= MIX["c"]:
                    act.wait_ge(c_normed, k - MIX["c"] + 1)
                nc.scalar.copy(h_hi[:, k, :], o_t[:, k, :]).then_inc(h_hi_ready, 1)
            for n in range(N_IN + 1, N_SPLIT):
                split_high(n)

            act.wait_ge(resid_ready, 2 * KD)
            for k in range(KD):
                m = KD + 3 + k
                if k >= 2:
                    act.wait_ge(sq_used, m - 1)
                nc.scalar.activation(sg[:, k % 2, :], resid[:, k, :], ACT.Square).then_inc(sq_ready, 1)
            act.wait_ge(sq_used, 2 * KD + 3)
            for b in range(2):
                nc.scalar.activation(std[:, HALF * b:HALF * b + HALF], bank[b][:, 0:HALF], ACT.Sqrt,
                                     scale=1.0 / D, bias=eps_col[:, 0:1]).then_inc(std_ready, 1)
            act.wait_ge(router_in, 32)
            nc.scalar.copy(r_hi[:, :, :], r_stage).then_inc(r_taken, 1)

            def gu_high(s, loads):
                act.wait_ge(gu_in[s], loads)
                nc.scalar.copy(gu_hi[:, s], gu_stage[:, s]).then_inc(gu_hi_ready, 1)

            def down_high(n_d, d, q, n_e):
                if d == 0:
                    act.wait_ge(d_in, 16 * q + 16)
                if not (isinstance(q, int) and q == 0 and d < 2):
                    act.wait_ge(down_full, n_d * 2 - 2)
                nc.scalar.copy(d_hi[:, d % 2, 0:n_e, :], d_stage[:, 0:n_e, P * d:P * d + P]).then_inc(d_hi_ready, 1)

            gu_high(0, 32)
            modulated(hidf, 3 * KD, KD, 2 * KD)
            act.wait_ge(r_full, 1)
            nc.scalar.activation(r_rows[:, :, 0, :], bank[7][:, 0:5 * N_EXPERTS].rearrange("p (t n) -> p t n", t=5),
                                 ACT.Sigmoid).then_inc(r_taken, 1)

            def silu(n, slot):
                for b in range(2):
                    act.wait_ge(au_full, n * 4 + b + 1)
                    nc.scalar.activation(sg[:, slot, HALF * b:HALF * b + HALF], bank[b][:, 0:HALF], ACT.Silu)\
                        .then_inc(sg_ready, 1)

            def hid_high(n, slot, e):
                for b in range(2):
                    act.wait_ge(hid_ready, n * 2 + b + 1)
                    nc.scalar.copy(hid_hi[:, e, HALF * b:HALF * b + HALF], hidf[:, slot, HALF * b:HALF * b + HALF])\
                        .then_inc(hid_hi_ready, 1)

            gu_high(1, 32)
            down_high(0, 0, 0, 1)
            down_high(1, 1, 0, 1)
            silu(0, 0)
            hid_high(0, 0, 0)
            for d in range(2, KD):
                down_high(d, d, 0, 1)

            def group(g, last):
                for e in range(GROUP):
                    n = g * GROUP + (1 + e)
                    slot = (1 + e) % 2
                    if e < GROUP - 1:
                        act.wait_ge(au_full, n * 4)
                        gu_high((2 + e) % 2, (g * 2 + 1 + (2 + e) // 2) * 32)
                    else:
                        down_high(g * KD + KD, 0, g + 1, GROUP)
                        down_high(g * KD + KD + 1, 1, g + 1, GROUP)
                    silu(n, slot)
                    if e == 0:
                        act.wait_ge(down_full, (g + 1) * 2 * KD)
                    hid_high(n, slot, e)
                for d in range(2, KD):
                    down_high(g * KD + (KD + d), d, g + 1, GROUP)
                    if d == 4 and not last:
                        act.wait_ge(au_full, (g * GROUP + GROUP) * 4)
                        gu_high(1, (g * 2 + 3) * 32)

            with act.Fori(0, N_GROUPS - 1) as g:
                group(g, False)
            group(N_GROUPS - 1, True)

            for k in range(KD):
                m = 2 * KD + 3 + k
                act.wait_ge(fin_ready, k + 1)
                if k >= 2:
                    act.wait_ge(sq_used, m - 1)
                nc.scalar.activation(sg[:, k % 2, :], resid[:, k, :], ACT.Square).then_inc(sq_ready, 1)
            act.wait_ge(sq_used, 3 * KD + 3)
            for b in range(2):
                nc.scalar.activation(std[:, HALF * b:HALF * b + HALF], bank[b][:, 0:HALF], ACT.Sqrt,
                                     scale=1.0 / D, bias=eps_col[:, 0:1]).then_inc(std_ready, 1)
            for t in range(5):
                n = tokens(t)[1]
                if t >= 2:
                    act.wait_ge(y_out[t % 2], 16 * (t // 2))
                for c in range(2):
                    m = 2 * t + c
                    act.wait_ge(y_full, m + 1)
                    nc.scalar.copy(y_acc_rows(t)[0:n, 512 * c:512 * c + 512], bank[2 + m % 4][0:n, :]).then_inc(y_taken, 1)

        @block.tensor
        def _(pe):
            mm = nc.tensor.matmul

            def three(out, hi_w, lo_w, hi_x, lo_x, first, last):
                mm(out, hi_w, hi_x, start=first, stop=False)
                mm(out, hi_w, lo_x, start=False, stop=False)
                return mm(out, lo_w, hi_x, start=False, stop=last)

            def halves(b):
                return slice(HALF * b, HALF * b + HALF)

            def mean_square(r, src, stat, width=KD):
                for k in range(width):
                    m = sq_base[r] + k
                    pe.wait_ge(sq_ready, m + 1)
                    for b in range(2):
                        ins = mm(bank[b][:, 0:HALF], stat, src[:, k % 2, halves(b)], start=(k == 0), stop=(k == width - 1))
                    ins.then_inc(sq_used, 1)

            def modulation(n):
                step = ("ada", n)
                tr.wait_free(pe, step)
                for i in range(4):
                    item = ("ada", 4 * n + i)
                    wait_stage(pe, item)
                    for k in range(KD):
                        ins = mm(tr_bank[tr.bank(step)][0:2, P * i:P * i + P], silu_c[:, k, :], staged(item)[:, k, :],
                                 start=(k == 0), stop=(k == KD - 1))
                    ins.then_inc(ada_rows, 1)

            def turn_modulation(n):
                pe.wait_ge(rows_copied, n + 1)
                for j in range(4):
                    ins = nc.tensor.transpose(tr_bank[tr.bank(("ada", n))][:, 2 * j:2 * j + 2],
                                              mod_rows[:, P * j:P * j + P], ident[0:2, 0:2])
                ins.then_inc(ada_full, 1)

            def project(n):
                pe.wait_ge(w_lo_ready, n + 1)
                for b in range(2):
                    if n < N_IN + 1:
                        if n:
                            pe.wait_ge(proj_taken, 2 * (n - 1) + b + 1)
                    else:
                        pe.wait_ge(resid_ready, 2 * (n - 1 - N_IN) + b + 1)
                    for k in range(KD):
                        if b == 0 and n == 0:
                            pe.wait_ge(h_lo_ready, k + 1)
                        if b == 0 and n == N_IN:
                            pe.wait_ge(h_lo_ready, KD + k + 1)
                        ins = three(bank[b][:, 0:HALF], w_hi[:, n % 2, k, :], w_lo[:, n % 2, k, :],
                                    h_hi[:, k, halves(b)], h_lo[:, k, halves(b)], k == 0, k == KD - 1)
                    ins.then_inc(proj_full, 1)

            pe.wait_ge(consts, 2)
            pe.wait_ge(vec_in, 6 * 16)
            nc.tensor.transpose(bank[7][:, 0:73], vec_rows[0:73, :], ident[0:73, 0:73]).then_inc(vec_turned, 1)
            for t in range(5):
                c0, n = tokens(t)
                if t:
                    if t == 1:
                        pe.wait_ge(silu_ready, 1)
                    modulation(t - 1)
                pe.wait_ge(x_in[t % 2], 16 * (t // 2 + 1))
                for c in range(2):
                    m = 2 * t + c
                    if m >= 3:
                        pe.wait_ge(xt_taken, m - 2)
                    for i in range(4):
                        k = 4 * c + i
                        ins = nc.tensor.transpose(bank[2 + m % 3][:, n * i:n * i + n], x_rows[0:n, t % 2, P * k:P * k + P],
                                                  ident[0:n, 0:n])
                    ins.then_inc(xt_full, 1)
                if t:
                    turn_modulation(t - 1)
            pe.wait_ge(xt_taken, 10)
            pe.wait_ge(consts, N_CONSTS)
            mean_square(0, sq, ones[:, :])
            pe.wait_ge(std_ready, 2)

            def turn_rows(step):
                n = step[1]
                name, j = TILES[n]
                src = feat(SLOT[name] + j) if name[0] == "k" else v_t[:, row_sources.index(n) % 2, :]
                r = {"wi": N_IDX, "ki": HD}.get(name, P)
                pe.wait_ge(proj_taken, 2 * n + 2)
                tr.wait_free(pe, step + (0,))
                b = tr.bank(step + (0,))
                for t in range(4):
                    ins = nc.tensor.transpose(tr_bank[b][:, r * t:r * t + r], src[0:r, P * t:P * t + P], ident[0:r, 0:r])
                ins.then_inc(tr_full[b], 1)
                tr.wait_free(pe, step + (1,))
                b = tr.bank(step + (1,))
                nc.tensor.transpose(tr_bank[b][0:N_SAMPLE, 0:r], src[0:r, N_PROMPT:NT], ident[0:r, 0:r])\
                    .then_inc(tr_full[b], 1)

            cache_value = {"i": 32, "a": 48, "b": 64, "c": 80}

            def wait_cached(g):
                for part in range(2 if g in "bc" else 1):
                    tr.wait_taken(pe, ("cache", g, part))

            def wait_rows(name):
                for st in rows_steps:
                    if TILES[st[1]][0] == name:
                        for half in range(2):
                            tr.wait_taken(pe, st + (half,))

            def key_products(out, q, k_new, k_old, t, key_ready):
                c0, rows = tokens(t)
                if t < 4:
                    return mm(out[:, 0:keys(t)], q[:, c0:c0 + rows], k_new[:, 0:keys(t)], start=True, stop=True)
                mm(out[0:rows, 0:PAST], q[:, c0:c0 + rows], k_old, start=True, stop=True)
                return mm(out[0:rows, PAST:N_KEYS_S], q[:, c0:c0 + rows], k_new[:, N_PROMPT:NT], start=True, stop=True)

            for step in SCHEDULE:
                kind, key = step[0], step[1:]
                if kind == "proj":
                    project(step[1])
                elif kind == "ada":
                    modulation(step[1])
                elif kind == "turn":
                    turn_modulation(step[1])
                elif kind == "rows":
                    turn_rows(step)
                elif kind == "cache":
                    g, part = key
                    pe.wait_ge(cache_in, cache_value[g])
                    tr.wait_free(pe, step)
                    b = tr.bank(step)
                    for i, (f, t) in enumerate(cache_blocks(g, part)):
                        ins = nc.tensor.transpose(tr_bank[b][:, P * i:P * i + P], cache_rows[:, t, P * f:P * f + P], ident[:, :])
                    ins.then_inc(tr_full[b], 1)
                elif kind == "score":
                    t, h = key
                    if t == 1 and h == 0:
                        pe.wait_ge(proj_taken, 2 * 6)
                        wait_cached("i")
                    r = slice(HD * (h % 2), HD * (h % 2) + HD)
                    qk.wait_free(pe, step)
                    b = qk.bank(step)
                    key_products(score_bank[b], feat(SLOT["qi"] + h // 2)[r, :], feat(SLOT["ki"])[r, :],
                                 cache_t[r, cache_slot("i"), 0, :], t, None).then_inc(qk_full[b], 1)
                elif kind == "qk":
                    g, h, t = key
                    if (g, h, t) == ("a", 0, 1):
                        wait_cached("a")
                        pe.wait_ge(proj_taken, 2 * 12)
                    if (g, h, t) == ("c", 0, 0):
                        wait_cached("c")
                        pe.wait_ge(proj_taken, 2 * N_IN)
                    w = HD if g == "a" else QK_C
                    for m in range(1 if g == "a" else 2):
                        r0 = HD * (h % 2) + w * m
                        r = slice(r0, r0 + w)
                        k = key + (m,)
                        qk.wait_free(pe, k)
                        b = qk.bank(k)
                        key_products(score_bank[b], feat(SLOT["q" + g] + h // 2)[r, :], feat(SLOT["k" + g] + h // 2)[r, :],
                                     cache_t[r, cache_slot(g), h // 2, :], t, None).then_inc(qk_full[b], 1)
                elif kind == "pt":
                    g, h, t = key
                    rows, n, u = tokens(t)[1], keys(t), unit_no[key]
                    pe.wait_ge(p_ready, u + 1)
                    tr.wait_free(pe, step)
                    b = tr.bank(step)
                    for j in range((n + P - 1) // P):
                        w = min(P, n - P * j)
                        ins = nc.tensor.transpose(tr_bank[b][0:w, rows * j:rows * j + rows],
                                                  p_work[0:rows, 2 * (u % 3), P * j:P * j + w], ident[0:rows, 0:rows])
                    ins.then_inc(tr_full[b], 1)
                elif kind == "pv":
                    g, h, t = key
                    rows, n, u = tokens(t)[1], keys(t), unit_no[key]
                    if (g, h, t) == ("a", 0, 1):
                        pe.wait_ge(v_cache_in, 16)
                        wait_rows("va")
                    if (g, h, t) == ("c", 0, 0):
                        pe.wait_ge(v_cache_in, 48)
                        wait_rows("vc")
                    tr.wait_taken(pe, ("pt",) + key)
                    if o_uses[step]:
                        pe.wait_ge(o_free, o_uses[step])
                    r = slice(HD * (h % 2), HD * (h % 2) + HD)
                    nb = (n + P - 1) // P
                    for j in range(nb):
                        w = min(P, n - P * j)
                        kt = j if t < 4 else (4 + j)
                        ins = mm(o_bank[r, 0:rows], v_of(g)[0:w, kt, HD * h:HD * h + HD], p_t[0:w, u % 2, j, 0:rows],
                                 start=(j == 0), stop=(j == nb - 1))
                    ins.then_inc(o_full, 1)
                elif kind == "z":
                    g, h, j = key
                    if (g, h, j) == ("b", 0, 3):
                        wait_cached("b")
                    qk.wait_free(pe, key)
                    b = qk.bank(key)
                    w = stick_width(key)
                    if g == "b":
                        r = slice(HD * (h % 2), HD * (h % 2) + HD)
                        ins = mm(score_bank[b][:, 0:w], feat(SLOT["kb"] + h // 2)[r, P * j:P * j + P],
                                 feat(SLOT["qb"] + h // 2)[r, P * j:N_PROMPT], start=True, stop=True)
                    else:
                        rows = stick_rows(key)
                        r = slice(HD * h, HD * h + HD)
                        for i in range(H_B // 2):
                            k_s = (feat(SLOT["kb"] + i)[r, N_PROMPT:NT] if j == 2
                                   else cache_t[r, cache_slot("b"), i, P * j:P * j + P])
                            ins = mm(score_bank[b][0:rows, HD * i:HD * i + HD], k_s,
                                     feat(SLOT["qb"] + i)[r, N_PROMPT:NT], start=(i == 0), stop=(i == H_B // 2 - 1),
                                     skip_group_check=True)
                    ins.then_inc(qk_full[b], 1)
                elif kind == "acc":
                    g, h, j = key
                    u, b = stick_no[key], qk.bank(key)
                    rows, w = stick_rows(key), stick_width(key)
                    pe.wait_ge(sp_ready, u + 1)
                    out = score_bank[b]
                    add = dict(start=False, skip_group_check=True)
                    mm(out[0:rows, 0:w], neg_tri[0:rows, 0:rows], sp_buf[0:rows, u % 3, 0:w], stop=False, **add)
                    if g == "b":
                        if j == 2:
                            mm(out[:, P:w], neg_ones[:, :], sp_buf[:, (u - 1) % 3, 0:w - P], stop=False, **add)
                        elif j < 2:
                            pe.wait_ge(run_ready, 2 * h + 2 - j)
                            mm(out[:, P:w], neg_ones[:, :], run[:, j, 0:w - P], stop=False, **add)
                        ins = mm(out[:, 0:P], ident[:, :], diag_neg[:, :], stop=True, **add)
                    else:
                        for back in range(1, 3 - j):
                            later = N_SAMPLE if j + back == 2 else P
                            ins = mm(out[0:rows, 0:w], neg_ones[0:later, 0:rows], sp_buf[0:later, (u - back) % 3, 0:w],
                                     stop=(j + back == 2), **add)
                        if j == 2:
                            ins = mm(out[0:rows, 0:w], ident[0:rows, 0:rows],
                                     diag_neg_s[:, :, :].rearrange("p h q -> p (h q)"), stop=True, **add)
                    ins.then_inc(qk_full[b], 1)
                elif kind == "av":
                    g, h, j = key
                    u = stick_no[key]
                    rows, w = stick_rows(key), stick_width(key)
                    qk.wait_taken(pe, key)
                    if (g, h, j) == ("b", 0, 3):
                        pe.wait_ge(v_cache_in, 32)
                        wait_rows("vb")
                    if (g == "b" and j == 3) or (g == "s" and j == 2):
                        use = o_uses[("av", g, h, 0)]
                        if use:
                            pe.wait_ge(o_free, use)
                    if g == "b":
                        r = slice(HD * (h % 2), HD * (h % 2) + HD)
                        ins = mm(o_bank[r, P * j:N_PROMPT], v_of(g)[:, j, HD * h:HD * h + HD], a_t[:, u % 2, 0:w],
                                 start=(j == 3), stop=(j == 0), skip_group_check=True)
                    else:
                        r = slice(HD * h, HD * h + HD)
                        for i in range(H_B // 2):
                            hh = 2 * i + h
                            ins = mm(o_bank[r, HD * i:HD * i + HD],
                                     v_of(g)[0:rows, 4 + j, HD * hh:HD * hh + HD], a_t[0:rows, u % 2, HD * i:HD * i + HD],
                                     start=(j == 2 and i == 0), stop=(j == 0 and i == H_B // 2 - 1),
                                     skip_group_check=True)
                    ins.then_inc(av_done, 1)

            for i in range(3):
                pe.wait_ge(sq_ready, KD + i + 1)
                if i:
                    pe.wait_ge(std_ready, 2 + 2 * i)
                else:
                    for b in range(2):
                        pe.wait_ge(qk_free[b], qk.uses[b])
                for b in range(2):
                    ins = mm(score_bank[b][:, 0:HALF], two_heads[:, :], sq[:, i % 2, halves(b)], start=True, stop=True)
                ins.then_inc(sq_used, 1)

            for n in range(N_IN, N_SPLIT):
                project(n)

            pe.wait_ge(resid_ready, 2 * KD)
            mean_square(1, sg, ones[:, :])
            pe.wait_ge(r_taken, 2)
            pe.wait_ge(h_lo_ready, 3 * KD)
            for t in range(5):
                c0 = P * t if t < 4 else NT - P
                for k in range(KD):
                    ins = three(bank[7][:, N_EXPERTS * t:N_EXPERTS * t + N_EXPERTS],
                                h_hi[:, k, c0:c0 + P], h_lo[:, k, c0:c0 + P], r_hi[:, k, :], r_lo[:, k, :],
                                k == 0, k == KD - 1)
            ins.then_inc(r_full, 1)

            def gate_up(n, slot, after):
                pe.wait_ge(gu_lo_ready, n + 1)
                for m in range(2):
                    for b in range(2):
                        if after:
                            pe.wait_ge(sg_ready if m == 0 else hid_ready, n * 2 + (b - 1))
                        for k in range(KD):
                            ins = three(bank[2 * m + b][:, 0:HALF], gu_hi[:, slot, m, k, :], gu_lo[:, slot, m, k, :],
                                        h_hi[:, k, halves(b)], h_lo[:, k, halves(b)], k == 0, k == KD - 1)
                        ins.then_inc(au_full, 1)

            def down(q, n_e, hid_before):
                for d in range(KD):
                    pe.wait_ge(d_lo_ready, q * KD + d + 1)
                    for b in range(2):
                        i = 2 * d + b
                        if not (isinstance(q, int) and q == 0 and i < 4):
                            pe.wait_ge(y_added, q * 2 * KD + (i - 3))
                        for e in range(n_e):
                            if d == 0:
                                pe.wait_ge(hid_lo_ready, hid_before + (2 * e + b + 1))
                            ins = three(bank[4 + i % 4][:, 0:HALF], d_hi[:, d % 2, e, :], d_lo[:, d % 2, e, :],
                                        hid_hi[:, e, halves(b)], hid_lo[:, e, halves(b)], e == 0, e == n_e - 1)
                        ins.then_inc(down_full, 1)

            pe.wait_ge(std_ready, 10)
            gate_up(0, 0, False)
            for t in range(5):
                c0 = P * t if t < 4 else NT - P
                pe.wait_ge(gates_ready, t + 1)
                if t >= 2:
                    pe.wait_ge(gates_copied, t - 1)
                nc.tensor.transpose(bank[4 + t % 2][0:N_EXPERTS, 0:P], r_rows[:, t, 2, :], ident[:, :]).then_inc(gates_turned, 1)
            pe.wait_ge(gated, 2 * GROUP)
            pe.wait_ge(r_taken, 3)
            down(0, 1, 0)

            def group(g):
                for e in range(GROUP):
                    gate_up(g * GROUP + (1 + e), (1 + e) % 2, True)
                down(g + 1, GROUP, g * 2 * GROUP + 2)

            with pe.Fori(0, N_GROUPS) as g:
                group(g)

            mean_square(2, sg, ones[:, :])
            for t in range(5):
                c0, n = tokens(t)
                for c in range(2):
                    m = 2 * t + c
                    if m == 0:
                        pe.wait_ge(std_ready, 12)
                    if m >= 4:
                        pe.wait_ge(y_taken, m - 3)
                    for i in range(4):
                        k = 4 * c + i
                        if t == 0:
                            pe.wait_ge(fin_ready, KD + k + 1)
                        ins = nc.tensor.transpose(bank[2 + m % 4][0:n, P * i:P * i + P], resid[:, k, c0:c0 + n], ident[:, :])
                    ins.then_inc(y_full, 1)

        @block.vector
        def _(dve):
            v = nc.vector
            n_step = 0

            def chain(ins):
                nonlocal n_step
                n_step += 1
                ins.then_inc(dve_step, 1)
                dve.wait_ge(dve_step, n_step)

            def copy_modulation(n):
                dve.wait_ge(ada_rows, 4 * n + 4)
                if n:
                    dve.wait_ge(ada_full, n)
                v.tensor_copy(mod_rows[:, :], tr_bank[tr.bank(("ada", n))][0:2, :]).then_inc(rows_copied, 1)

            def modulation(n):
                step = ("ada", n)
                dve.wait_ge(ada_full, n + 1)
                part = tr_bank[tr.bank(step)][:, 0:8].rearrange("p (e b) -> p e b", b=2)
                add1 = 1.0 if n in (2, 3, 8, 9) else 0.0
                for b in range(2):
                    ins = v.scalar_tensor_tensor(out=mod[:, 4 * n:4 * n + 4, b], in0=part[:, :, b], scalar=add1,
                                                 in1=vec[:, 4 * n:4 * n + 4], op0=ALU.add, op1=ALU.add)
                tr.take(ins, step)

            def normed(src, dst, inc):
                for k in range(KD + 1):
                    if k < KD:
                        if k >= 2:
                            dve.wait_ge(h_lo_ready, inc + k - 1)
                        v.tensor_tensor(dst[:, k % 2, :], src[:, k, :], rstd[:, :], ALU.mult).then_inc(norm_ready, 1)
                    if k:
                        low(dst[:, (k - 1) % 2, :], k - 1, inc)

            def low(src, k, base):
                dve.wait_ge(h_hi_ready, base + k + 1)
                v.tensor_tensor(h_lo[:, k, :], src, h_hi[:, k, :].bitcast(F32), ALU.subtract).then_inc(h_lo_ready, 1)

            def invert_std(value):
                dve.wait_ge(std_ready, value)
                v.reciprocal(rstd[:, :], std[:, :]).then_inc(rstd_ready, 1)



            dve.wait_ge(vec_turned, 1)
            v.tensor_copy(vec[:, :], bank[7][:, 0:73]).then_inc(vec_ready, 1)

            for t in range(5):
                c0, n = tokens(t)
                if t:
                    copy_modulation(t - 1)
                    modulation(t - 1)
                for c in range(2):
                    m = 2 * t + c
                    dve.wait_ge(xt_full, m + 1)
                    v.tensor_copy(o_t[:, 4 * c:4 * c + 4, c0:c0 + n],
                                  bank[2 + m % 3][:, 0:4 * n].rearrange("p (k t) -> p k t", k=4)).then_inc(xt_taken, 1)
            split_low(dve, v, 0)
            dve.wait_ge(consts, N_CONSTS)
            chain(v.scalar_tensor_tensor(out=dist[:, :], in0=dist[:, :], scalar=-1.0, in1=dist[:, :], op0=ALU.mult,
                                         op1=ALU.max))
            chain(v.memset(dist[0:CHUNK, 512 - CHUNK:512], -NEG))
            dve.wait_ge(lam_in, 16)
            for i in range(2):
                a = lam_rows[:, 2 * QK_C * i:2 * QK_C * i + QK_C]
                b = lam_rows[:, 2 * QK_C * i + QK_C:2 * QK_C * (i + 1)]
                v.tensor_tensor_reduce(out=a, in0=a, in1=b, scale=1.0, scalar=0.0, op0=ALU.mult, op1=ALU.add,
                                       accum_out=lam_dot[:, i:i + 1]).then_inc(lam_dots, 1)
            invert_std(2)
            dve.wait_ge(rstd_ready, 1)
            normed(o_t, hf, 0)
            dve.wait_ge(lam_exps, 1)
            chain(v.memset(lam_fac[:, 0:1], 1.0))
            chain(v.tensor_tensor(lam_fac[:, 1:2], lam_exp[:, 0:1], lam_exp[:, 1:2], ALU.subtract))
            chain(v.tensor_scalar(lam_fac[:, 1:2], lam_fac[:, 1:2], LAM_INIT, None, ALU.add))

            for step in SCHEDULE:
                kind, key = step[0], step[1:]
                if kind == "proj" and vector_splits(step):
                    dve.wait_ge(w_lo_ready, step[1] + 1)
                    split_low(dve, v, step[1] + 1)
                if kind == "ada":
                    copy_modulation(step[1])
                elif kind == "turn":
                    modulation(step[1])
                elif kind == "score":
                    t, h = key
                    n, m, rows = keys(t), score_no[step], tokens(t)[1]
                    if m == 0:
                        for half in range(2):
                            tr.wait_taken(dve, ("rows", 1, half))
                    qk.wait_taken(dve, step)
                    rel, w, out = bias[0:rows, m % 2, 0:n], wi_rows[0:rows, t, h:h + 1], pick[t][0:rows, :]
                    if h == 0:
                        v.tensor_scalar(out, rel, w, None, ALU.mult).then_inc(score_ready, 1)
                    else:
                        dve.wait_ge(score_ready, m)
                        v.scalar_tensor_tensor(out=out, in0=rel, scalar=w, in1=out, op0=ALU.mult, op1=ALU.add)\
                            .then_inc(score_ready, 1)
                elif kind == "topk":
                    t = step[1]
                    rows, n = tokens(t)[1], keys(t)
                    s = pick[t][0:rows, :]
                    dve.wait_ge(score_ready, score_no[("score", t, N_IDX - 1)] + 1)
                    if t < 4:
                        chain(v.memset(pick[t][0:CHUNK, n - CHUNK:n], INVALID))
                    for _ in range((TOPK_PROMPT if t < 4 else TOPK_SAMPLE) // 8):
                        chain(v.max(max8[0:rows, :], s))
                        chain(v.match_replace(s, max8[0:rows, :], s, CHOSEN))
                    v.tensor_scalar(s, s, (CHOSEN + INVALID) / 2, NEG, ALU.is_gt, ALU.mult).then_inc(picked, 1)
                elif kind == "max":
                    g, h, t = key
                    rows, n, u = tokens(t)[1], keys(t), unit_no[key]
                    d0 = DIST0 - P * t if t < 4 else DIST0 - PAST
                    if g == "a":
                        slot, scale = u % 2, SCALE_A
                        tab = bias[0:rows, slot, 0:n]
                        dr = dist[0:rows, d0:d0 + n]
                        if u >= 2:
                            qk.wait_taken(dve, unit_key[u - 2] + (0,))
                        if t:
                            dve.wait_ge(picked, t)
                            chain(v.scalar_tensor_tensor(out=tab, in0=dr, scalar=-SLOPE_A[h] / SCALE_A,
                                                         in1=pick[t][0:rows, :], op0=ALU.mult, op1=ALU.add))
                        else:
                            chain(v.tensor_scalar(tab, dr, -SLOPE_A[h] / SCALE_A, None, ALU.mult))
                    else:
                        slot, scale = h % 2, SCALE_C
                        dve.wait_ge(bias_ready, h + 1)
                        tab = bias[0:rows, slot, d0:d0 + n]
                    if u >= 3:
                        tr.wait_full(dve, ("pt",) + unit_key[u - 3])
                        dve.wait_ge(p_ready, u - 2)
                    for m in range(2 if g == "c" else 1):
                        k = key + (m,)
                        qk.wait_full(dve, k)
                        qk.take(v.tensor_tensor_reduce(out=p_work[0:rows, 2 * (u % 3) + m, 0:n],
                                                       in0=score_bank[qk.bank(k)][0:rows, 0:n], in1=tab,
                                                       scale=-scale, scalar=3e38, op0=ALU.add, op1=ALU.min,
                                                       accum_out=n_max[0:rows, u % 2, m:m + 1]), k)
                elif kind == "norm":
                    g, h, t = key
                    rows, n, u = tokens(t)[1], keys(t), unit_no[key]
                    maps = 2 if g == "c" else 1
                    dve.wait_ge(exp_ready, map_no[key + (maps - 1,)] + 1)
                    e = [p_work[0:rows, 2 * (u % 3) + m, 0:n] for m in range(2)]
                    rec = p_rec[0:rows, u % 2, :]
                    if u >= 2:
                        dve.wait_ge(p_ready, u - 1)
                    chain(v.reciprocal(rec[:, 0:maps], p_sum[0:rows, u % 2, 0:maps]))
                    if g == "a":
                        v.tensor_scalar(e[0], e[0], rec[:, 0:1], None, ALU.mult).then_inc(p_ready, 1)
                    else:
                        chain(v.tensor_tensor(rec, rec, lam_fac[0:rows, :], ALU.mult))
                        chain(v.tensor_scalar(e[1], e[1], rec[:, 1:2], None, ALU.mult))
                        v.scalar_tensor_tensor(out=e[0], in0=e[0], scalar=rec[:, 0:1], in1=e[1], op0=ALU.mult,
                                               op1=ALU.subtract).then_inc(p_ready, 1)
                elif kind == "pv":
                    g, h, t = key
                    c0, rows = tokens(t)
                    if unit_no[key] == 0:
                        dve.wait_ge(spilled, 16)
                    r = slice(HD * (h % 2), HD * (h % 2) + HD)
                    dve.wait_ge(o_full, unit_no[key] + 1)
                    v.tensor_copy(o_t[r, MIX[g] + h // 2, c0:c0 + rows], o_bank[r, 0:rows]).then_inc(o_free, 1)
                elif kind == "z":
                    rows, w, u = stick_rows(key), stick_width(key), stick_no[key]
                    qk.wait_full(dve, key, 1)
                    if u == 0:
                        dve.wait_ge(o_full, unit_no[last_a_pv[1:]] + 1)
                    if u >= 2:
                        dve.wait_ge(sp_ready, u - 1)
                    v.tensor_scalar(l_buf[0:rows, u % 2, 0:w], score_bank[qk.bank(key)][0:rows, 0:w], BIG_Z, None,
                                    ALU.min).then_inc(capped, 1)
                elif kind == "sp":
                    g, h, j = key
                    rows, w, u = stick_rows(key), stick_width(key), stick_no[key]
                    dve.wait_ge(l_ready, u + 1)
                    if u >= 2:
                        qk.wait_full(dve, stick_key[u - (1 if g == "s" else 2)], 2)
                    sums = len([k for k in list(stick_no)[:max(u - 1, 0)] if k[0] == "b" and k[2] in (1, 2)])
                    if sums:
                        dve.wait_ge(run_ready, sums)
                    sp = sp_buf[0:rows, u % 3, :]
                    ins = v.tensor_tensor(sp[:, 0:w], score_bank[qk.bank(key)][0:rows, 0:w], l_buf[0:rows, u % 2, 0:w],
                                          ALU.max)
                    if g == "b":
                        chain(ins)
                        ins = v.tensor_tensor(sp[:, 0:P], sp[:, 0:P], diag_01[:, :], ALU.mult)
                    elif j == 2:
                        chain(ins)
                        ins = v.tensor_tensor(sp[:, 0:w], sp[:, 0:w], diag_01_s[:, :, :].rearrange("p h q -> p (h q)"),
                                              ALU.mult)
                    ins.then_inc(sp_ready, 1)
                    if g == "b" and j in (1, 2):
                        dve.wait_ge(sp_ready, u + 1)
                        later = sp_buf[:, (u - 1) % 3, 0:P] if j == 2 else run[:, 1, 0:2 * P]
                        if j == 1:
                            dve.wait_ge(run_ready, 2 * h + 1)
                        chain(v.tensor_copy(run[:, j - 1, 0:P], sp[:, 0:P]))
                        v.tensor_tensor(run[:, j - 1, P:w], sp[:, P:w], later, ALU.add).then_inc(run_ready, 1)
                elif kind == "av" and key[2] == 0:
                    g, h, j = key
                    dve.wait_ge(av_done, stick_no[key] + 1)
                    if g == "b":
                        r = slice(HD * (h % 2), HD * (h % 2) + HD)
                        dst, src = o_t[r, MIX["b"] + h // 2, 0:N_PROMPT], o_bank[r, 0:N_PROMPT]
                    else:
                        r = slice(HD * h, HD * h + HD)
                        dst = o_t[r, MIX["b"]:MIX["c"], N_PROMPT:NT]
                        src = o_bank[r, 0:3 * N_SAMPLE].rearrange("p (i q) -> p i q", i=3)
                    v.tensor_copy(dst, src).then_inc(o_free, 1)

            for i in range(3):
                o = o_t[:, MIX["c"] + i, :]
                invert_std(4 + 2 * i)
                dve.wait_ge(rstd_ready, 2 + i)
                chain(v.tensor_tensor(o, o, rstd[:, :], ALU.mult))
                v.tensor_scalar(o, o, vec[:, 72:73], 1.0 - LAM_INIT, ALU.mult, ALU.mult).then_inc(c_normed, 1)
            for k in range(KD):
                low(o_t[:, k, :], k, KD)

            dve.wait_ge(resid_in, 16)
            for n in range(4, 12):
                tr.wait_taken(dve, ("ada", n))
            for e in range(KD):
                n = N_IN + e
                if e < KD - 1:
                    split_low(dve, v, n + 1)
                for b in range(2):
                    dve.wait_ge(proj_full, 2 * n + b + 1)
                    parts = [(0, HALF, 0)] if b == 0 else [(HALF, N_PROMPT, 0), (N_PROMPT, NT, 1)]
                    for a, z, stream in parts:
                        r = resid[:, e, a:z]
                        ins = v.scalar_tensor_tensor(out=r, in0=bank[b][:, a - HALF * b:z - HALF * b],
                                                     scalar=mod[:, 2 * KD + e, stream:stream + 1], in1=r,
                                                     op0=ALU.mult, op1=ALU.add)
                    ins.then_inc(resid_ready, 1)

            dve.wait_ge(router_in, 32)
            dve.wait_ge(r_taken, 1)
            v.tensor_tensor(r_lo[:, :, :], r_stage, r_hi[:, :, :].bitcast(F32), ALU.subtract).then_inc(r_taken, 1)

            def gu_low(n, s):
                dve.wait_ge(gu_hi_ready, n + 1)
                v.tensor_tensor(gu_lo[:, s], gu_stage[:, s], gu_hi[:, s].bitcast(F32), ALU.subtract)\
                    .then_inc(gu_lo_ready, 1)

            def down_low(n_d, d, n_e):
                dve.wait_ge(d_hi_ready, n_d + 1)
                v.tensor_tensor(d_lo[:, d % 2, 0:n_e, :], d_stage[:, 0:n_e, P * d:P * d + P],
                                d_hi[:, d % 2, 0:n_e, :].bitcast(F32), ALU.subtract).then_inc(d_lo_ready, 1)

            def hidden(n, slot, e, routed):
                hv = [slice(HALF * b, HALF * b + HALF) for b in range(2)]
                if routed:
                    g = routed[0]
                    dve.wait_ge(g_in[e], g * 16 + 16)
                    for b in range(2):
                        dve.wait_ge(sg_ready, n * 2 + (b + 1))
                        v.tensor_tensor(sg[:, slot, hv[b]], sg[:, slot, hv[b]], gate_bc[:, e, hv[b]], ALU.mult)\
                            .then_inc(gated, 1)
                for b in range(2):
                    if routed:
                        dve.wait_ge(gated, n * 2 + (2 * GROUP - 2 + b + 1))
                    else:
                        dve.wait_ge(sg_ready, n * 2 + (b + 1))
                    dve.wait_ge(au_full, n * 4 + (2 + b + 1))
                    if routed:
                        dve.wait_ge(hid_lo_ready, n * 2)
                    v.tensor_tensor(hidf[:, slot, hv[b]], sg[:, slot, hv[b]], bank[2 + b][:, 0:HALF], ALU.mult)\
                        .then_inc(hid_ready, 1)
                for b in range(2):
                    dve.wait_ge(hid_hi_ready, n * 2 + (b + 1))
                    v.tensor_tensor(hid_lo[:, e, hv[b]], hidf[:, slot, hv[b]], hid_hi[:, e, hv[b]].bitcast(F32),
                                    ALU.subtract).then_inc(hid_lo_ready, 1)

            def add_y(q, d, first):
                for b in range(2):
                    i = 2 * d + b
                    dve.wait_ge(down_full, q * 2 * KD + (i + 1))
                    y, part = y_acc[:, d, HALF * b:HALF * b + HALF], bank[4 + i % 4][:, 0:HALF]
                    if first:
                        ins = v.tensor_copy(y, part)
                    else:
                        dve.wait_ge(y_added, q * 2 * KD + (i - 2 * KD + 1))
                        ins = v.tensor_tensor(y, part, y, ALU.add)
                    ins.then_inc(y_added, 1)

            invert_std(10)
            dve.wait_ge(rstd_ready, 5)
            normed(resid, hidf, 2 * KD)
            gu_low(0, 0)

            dve.wait_ge(r_taken, 3)
            for t in range(5):
                s, sb_, gt = (r_rows[:, t, i, :] for i in range(3))
                chain(v.tensor_tensor(sb_, s, b_rows[:, :], ALU.add))
                chain(v.max(r_max[:, t, :], sb_))
                chain(v.match_replace(sb_, r_max[:, t, :], sb_, CHOSEN))
                chain(v.scalar_tensor_tensor(out=gt, in0=sb_, scalar=(CHOSEN + INVALID) / 2, in1=s, op0=ALU.is_lt,
                                             op1=ALU.mult, accum_out=r_sum[:, t, 0:1]))
                chain(v.reciprocal(r_sum[:, t, 1:2], r_sum[:, t, 0:1]))
                v.tensor_scalar(gt, gt, r_sum[:, t, 1:2], ROUTED_SCALE, ALU.mult, ALU.mult).then_inc(gates_ready, 1)
            gu_low(1, 1)
            down_low(0, 0, 1)
            down_low(1, 1, 1)
            for t in range(5):
                c0 = P * t if t < 4 else NT - P
                dve.wait_ge(gates_turned, t + 1)
                if t == 4:
                    dve.wait_ge(gates_copied, 4)
                ins = v.tensor_copy(gate_t[:, c0:c0 + P], bank[4 + t % 2][0:N_EXPERTS, 0:P])
                if t < 4:
                    ins.then_inc(gates_copied, 1)
                else:
                    ins.then_inc(gated, 2 * GROUP)
            dve.wait_ge(h_lo_ready, 3 * KD)
            hidden(0, 0, 0, None)
            for d in range(KD):
                add_y(0, d, True)
                if d + 2 < KD:
                    down_low(d + 2, d + 2, 1)

            def group(g, last):
                for e in range(GROUP):
                    n = g * GROUP + (1 + e)
                    if e < GROUP - 1:
                        gu_low(n + 1, (2 + e) % 2)
                    else:
                        down_low(g * KD + KD, 0, GROUP)
                        down_low(g * KD + (KD + 1), 1, GROUP)
                    hidden(n, (1 + e) % 2, e, (g,))
                for d in range(KD):
                    add_y(g + 1, d, False)
                    if d + 2 < KD:
                        down_low(g * KD + (KD + d + 2), d + 2, GROUP)
                    if d == 2 and not last:
                        gu_low(g * GROUP + (GROUP + 1), 1)

            with dve.Fori(0, N_GROUPS - 1) as g:
                group(g, False)
            group(N_GROUPS - 1, True)

            dve.wait_ge(y_added, (N_GROUPS + 1) * 2 * KD)
            for k in range(KD):
                for b, (a, z) in enumerate(((0, N_PROMPT), (N_PROMPT, NT))):
                    r = resid[:, k, a:z]
                    ins = v.scalar_tensor_tensor(out=r, in0=y_acc[:, k, a:z], scalar=mod[:, 5 * KD + k, b:b + 1], in1=r,
                                                 op0=ALU.mult, op1=ALU.add)
                ins.then_inc(fin_ready, 1)
            invert_std(12)
            dve.wait_ge(rstd_ready, 6)
            dve.wait_ge(fin_ready, KD)
            for k in range(KD):
                r = resid[:, k, :]
                chain(v.tensor_tensor(r, r, rstd[:, :], ALU.mult))
                v.tensor_scalar(r, r, vec[:, 6 * KD + k:6 * KD + k + 1], None, ALU.mult).then_inc(fin_ready, 1)


OUTPUTS = {
    "y_prompt": (1, N_PROMPT, D), "y_sample": (1, N_SAMPLE, D),
    "kv_a_p": (1, 1, N_PROMPT, 2, H_A, HD), "ki_p": (1, 1, N_PROMPT, HD),
    "kv_b_p": (1, 1, N_PROMPT, 2, H_B, HD), "kv_c_p": (1, 1, N_PROMPT, 2, H_C, HD),
    "kv_a_s": (1, 1, N_SAMPLE, 2, H_A, HD), "ki_s": (1, 1, N_SAMPLE, HD),
    "kv_b_s": (1, 1, N_SAMPLE, 2, H_B, HD), "kv_c_s": (1, 1, N_SAMPLE, 2, H_C, HD),
}


def kernel(**inputs):
    import numpy as np
    import concourse.bacc as bacc
    from concourse.bass_utils import run_bass_kernel_spmd

    nc = bacc.Bacc("TRN2", target_bir_lowering=False, num_devices=1)
    io, arrays = {}, {}
    for name, value in inputs.items():
        a = np.ascontiguousarray(value)
        arrays[f"in_{name}"] = a
        io[name] = nc.dram_tensor(f"in_{name}", a.shape, mybir.dt.from_np(a.dtype), kind="ExternalInput").ap()
    for name, shape in OUTPUTS.items():
        ap = nc.dram_tensor(f"out_{name}", shape, F32, kind="ExternalOutput").ap()
        if name.startswith("kv"):
            ap = ap[0, 0].rearrange("t kv h d -> t kv (h d)")
        elif name.startswith("ki"):
            ap = ap[0, 0]
        io[name] = ap
    build(nc, io)
    r = run_bass_kernel_spmd(nc, [arrays], core_ids=[0])
    return tuple(r.results[0][f"out_{name}"] for name in OUTPUTS)
```

```python
from contextlib import ExitStack

import concourse.bass as bass
from concourse import mybir

F32 = mybir.dt.float32
F32R = mybir.dt.float32r
ALU = mybir.AluOpType
ACT = mybir.ActivationFunctionType

P = 128
D = 1024
KD = D // P
N_PROMPT, N_SAMPLE, PAST = 512, 64, 256
NT = N_PROMPT + N_SAMPLE
HALF = NT // 2
N_KEYS_S = PAST + N_SAMPLE
CHUNK = 64
HD = 64
H_A, H_B, H_C = 4, 6, 6
QK_C = HD // 2
N_IDX = 8
TOPK_PROMPT, TOPK_SAMPLE = 128, 80
N_EXPERTS = 64
TOP_K = 8
F = D // 8
GROUP = 4
N_GROUPS = N_EXPERTS // GROUP
ROUTED_SCALE = 2.5
EPS = 1e-6
LAM_INIT = 0.8 - 0.6
SLOPE_A = [2.0 ** (-8.0 * (i + 1) / H_A) for i in range(H_A)]
SLOPE_C = [2.0 ** (-8.0 * (i + 1) / H_C) for i in range(H_C)]
SCALE_A = HD ** -0.5
SCALE_C = QK_C ** -0.5
BIG_Z = 30.0
NEG = -1e30
INVALID = -3e38
CHOSEN = -3.3e38
DIST0 = 384

COL = {"qa": 0, "ka": 256, "va": 512, "qi": 768, "ki": 1280, "wi": 1344,
       "qb": 1352, "kb": 1736, "vb": 2120, "qc": 2504, "kc": 2888, "vc": 3272}
TILES = ([("ki", 0), ("wi", 0)] + [("qi", i) for i in range(4)]
         + [(n, i) for n in ("qa", "ka", "va") for i in range(2)]
         + [(n, i) for n in ("qb", "kb", "vb", "qc", "kc", "vc") for i in range(3)])
N_IN = len(TILES)
SLOT = {"ki": 0, "qi": 1, "qa": 6, "ka": 8, "qb": 10, "kb": 13, "qc": 0, "kc": 3}
ROWS = ("ki", "wi", "ka", "va", "kb", "vb", "kc", "vc")
MIX = {"a": 0, "b": 2, "c": 5}


def tokens(t):
    return (P * t, P) if t < 4 else (N_PROMPT, N_SAMPLE)


def keys(t):
    return P * (t + 1) if t < 4 else N_KEYS_S


def make_schedule():
    tile = {n: i for i, n in enumerate(TILES)}
    s = []
    ada = iter(range(4, 12))

    def project(names):
        for k in names:
            s.append(("proj", tile[k]))
            if k[0] in ROWS:
                s.append(("rows", tile[k]))

    def project_with_ada(k):
        n = next(ada, None)
        s.extend([("ada", n), ("proj", tile[k]), ("turn", n)] if n is not None else [("proj", tile[k])])
        if k[0] in ROWS:
            s.append(("rows", tile[k]))

    project(TILES[:6])
    s.append(("cache", "i", 0))
    tiles = list(TILES[6:21])
    for t in (1, 2, 3, 4):
        for h in range(N_IDX):
            s.append(("score", t, h))
        s.append(("topk", t))
        for _ in range((3, 3, 4, 2)[t - 1]):
            project([tiles.pop(0)])
    s.append(("cache", "a", 0))
    for k in tiles:
        project_with_ada(k)
    s += [("cache", "b", 0), ("cache", "b", 1)]

    def softmax_units(units, fill=()):
        fill, norms, split = list(fill), [], 0
        n = len(units)
        for i in range(n + 3):
            m = next(ada, None) if i % 4 == 0 and units[0][0] == "a" else None
            if m is not None:
                s.append(("ada", m))
            if i == 0:
                s.extend([("pad",) + units[0], ("pad",) + units[1]])
            if i < n:
                s.append(("qk",) + units[i])
                if i + 2 < n:
                    s.append(("pad",) + units[i + 2])
                s.append(("max",) + units[i])
            if m is not None:
                s.append(("turn", m))
            if 1 <= i <= n:
                s.append(("norm",) + units[i - 1])
            if fill and i % 2 == 1:
                project([fill.pop(0)])
            if 2 <= i <= n + 1:
                s.append(("pt",) + units[i - 2])
            if i >= 3:
                s.append(("pv",) + units[i - 3])
                last = units[i - 3]
                if last[0] == "c" and last[1] % 2 and last[2] == 4:
                    s.append(("square", last[1] // 2))
                    norms = [("means", last[1] // 2), ("root", last[1] // 2), ("split_o", MIX["c"] + last[1] // 2)]
                    if i == n + 2:
                        s.extend(norms)
                elif norms:
                    s.append(norms.pop(0))
                elif last[0] == "c" and split < MIX["c"]:
                    s.append(("split_o", split))
                    split += 1
                    if split == 1:
                        s.append(("split_w", N_IN + 1))
        for k in fill:
            project([k])

    softmax_units([("a", h, t) for t in (1, 2, 3, 4, 0) for h in range(H_A)], TILES[21:27])
    s += [("cache", "c", 0), ("cache", "c", 1)]
    units = [("b", h, j) for h in range(H_B) for j in (3, 2, 1, 0)] \
        + [("s", par, j) for par in (0, 1) for j in (2, 1, 0)]
    s += [("pad",) + units[0], ("pad",) + units[1]]
    project(TILES[27:])
    for i in range(len(units) + 4):
        if 3 <= i <= len(units) + 2:
            s.append(("acc",) + units[i - 3])
        if i < len(units):
            s.append(("z",) + units[i])
            if 1 < i + 1 < len(units) and units[i + 1][0] == "b":
                s.append(("pad",) + units[i + 1])

        if 1 <= i <= len(units):
            s.append(("sp",) + units[i - 1])
        if i >= 4:
            s.append(("av",) + units[i - 4])

    assert next(ada, None) is None
    softmax_units([("c", h, t) for h in range(H_C) for t in range(5)])
    return s


SCHEDULE = make_schedule()
PROLOGUE = [("x", 0), ("x", 1), ("ada", 0), ("x", 2), ("turn", 0), ("x", 3), ("ada", 1), ("x", 4), ("turn", 1),
            ("sum", 0), ("ada", 2), ("means", 0), ("turn", 2), ("norm", 0), ("ada", 3), ("turn", 3), ("norm", 4)]


class Ring:

    def __init__(self, size, full, free):
        self.size, self.full, self.free = size, full, free
        self.n, self.fills, self.uses = 0, [0] * size, [0] * size
        self.at = {}

    def use(self, key, fills=1, among=None):
        b = self.n % (among or self.size)
        self.n += 1
        self.at[key] = (b, self.uses[b], self.fills[b])
        self.fills[b] += fills
        self.uses[b] += 1

    def bank(self, key):
        return self.at[key][0]

    def wait_free(self, eng, key):
        b, before, _ = self.at[key]
        if before:
            eng.wait_ge(self.free[b], before)

    def wait_full(self, eng, key, fill=1):
        b, _, fills = self.at[key]
        eng.wait_ge(self.full[b], fills + fill)

    def wait_taken(self, eng, key):
        b, before, _ = self.at[key]
        eng.wait_ge(self.free[b], before + 1)

    def fill(self, ins, key):
        ins.then_inc(self.full[self.at[key][0]], 1)

    def take(self, ins, key):
        ins.then_inc(self.free[self.at[key][0]], 1)


def build(nc, io):
    ctx = ExitStack()
    with ctx:
        def sb(name, shape, dt=F32, stack=ctx):
            return stack.enter_context(nc.sbuf_tensor(name, shape, dt))

        def sem(name):
            return ctx.enter_context(nc.semaphore(name))

        bank = [ctx.enter_context(nc.psum_tensor(f"bank{i}", [P, 512], F32)) for i in range(8)]
        x_spill = nc.dram_tensor("x_spill", (P, KD, NT), F32).ap()
        gate_rows = nc.dram_tensor("gate_rows", (N_EXPERTS, NT), F32).ap()

        resid = sb("resid", [P, KD, NT])
        h_hi = sb("h_hi", [P, KD, NT], F32R)
        h_lo = sb("h_lo", [P, KD, NT], F32R)
        ident = sb("ident", [P, P])
        ones = sb("ones", [P, P])
        vec = sb("vec", [P, 73])
        silu_c = sb("silu_c", [P, KD, 2])
        mod = sb("mod", [P, 6 * KD, 2])
        log_ms = sb("log_ms", [P, NT])
        rstd = sb("rstd", [P, NT])
        vec_rows = rstd[0:73, 0:P]
        eps_col = sb("eps_col", [P, 1])

        early = ExitStack()
        ea = lambda name, shape, dt=F32: sb(name, shape, dt, early)
        feat2 = ea("feat2", [P, 8, NT])
        o_t = ea("o_t", [P, KD, NT])
        v_t = ea("v_t", [P, 2, NT])
        pro = ExitStack()
        hf = sb("hf", [P, 2, NT], F32, pro)
        sq = sb("sq", [P, 2, NT], F32, pro)
        x_rows = sb("x_rows", [P, 2, D], F32, pro)
        pro.close()
        v_rows = [ea(f"v_rows{i}", [P, 7, 384]) for i in range(2)]
        cache_rows = ea("cache_rows", [P, 2, 384])
        cache_t = ea("cache_t", [P, 2, 3, PAST])
        pick_stack = ExitStack()
        pick = {t: sb(f"pick{t}", [P, keys(t)], F32, pick_stack) for t in (1, 2, 3, 4)}
        pick_stack.close()
        sp_buf = ea("sp_buf", [P, 3, 512])
        w_stage = ea("w_stage", [P, 4, KD, P])
        w_hi = ea("w_hi", [P, 2, KD, P], F32R)
        w_lo = ea("w_lo", [P, 2, KD, P], F32R)
        k_rows = ea("k_rows", [P, 2, 5, P])
        wi_rows = ea("wi_rows", [P, 5, N_IDX])
        neg_tri = ea("neg_tri", [P, P])
        neg_ones = ea("neg_ones", [P, P])
        diag_neg = ea("diag_neg", [P, P])
        diag_01 = ea("diag_01", [P, P])
        diag_neg_s = ea("diag_neg_s", [N_SAMPLE, H_B // 2, N_SAMPLE])
        diag_01_s = ea("diag_01_s", [N_SAMPLE, H_B // 2, N_SAMPLE])
        two_heads = ea("two_heads", [P, P])
        dist = ea("dist", [P, 512])
        lam_rows = ea("lam_rows", [P, 4 * QK_C])
        lam_dot = ea("lam_dot", [P, 2])
        lam_exp = ea("lam_exp", [P, 2])
        lam = ea("lam", [P, 1])
        max8 = ea("max8", [P, 8])
        bias = ea("bias", [P, 2, 512])
        p_work = ea("p_work", [P, 6, 512])
        turned = ExitStack()
        p_t = sb("p_t", [P, 2, 4, P], F32, turned)
        turned.close()
        l_buf = ea("l_buf", [P, 2, 512])
        n_max = ea("n_max", [P, 2, 2])
        p_sum = ea("p_sum", [P, 2, 2])
        p_rec = ea("p_rec", [P, 2, 2])
        run = ea("run", [P, 2, 384])
        a_t = ea("a_t", [P, 2, 512])
        early.close()
        q_pad = a_t[:, :, :].rearrange("p s (b c) -> p (s b) c", c=P)
        k_pad = bias[:, 0, :].rearrange("p (b c) -> p b c", c=P)
        mod_rows = run[0:2, :, :].rearrange("p s c -> p (s c)")[:, 0:512]
        c_sq = sp_buf[:, :, :].rearrange("p s c -> p (s c)")[:, 0:NT]

        late = ExitStack()
        la = lambda name, shape, dt=F32: sb(name, shape, dt, late)
        y_acc = la("y_acc", [P, KD, NT])
        r_max = la("r_max", [P, 5, 8])
        r_sum = la("r_sum", [P, 5, 2])
        row_root = la("row_root", [P, 5])
        row_rstd = la("row_rstd", [P, 5])
        b_rows = la("b_rows", [P, N_EXPERTS])
        gu_stage = la("gu_stage", [P, 2, 2, KD, F])
        gu_hi = la("gu_hi", [P, 2, 2, KD, F], F32R)
        gu_lo = la("gu_lo", [P, 2, 2, KD, F], F32R)
        d_stage = la("d_stage", [P, GROUP, D])
        d_hi = la("d_hi", [P, 2, GROUP, P], F32R)
        d_lo = la("d_lo", [P, 2, GROUP, P], F32R)
        hid_hi = la("hid_hi", [P, GROUP, NT], F32R)
        hid_lo = la("hid_lo", [P, GROUP, NT], F32R)
        gate_bc = la("gate_bc", [P, GROUP, NT])
        sg = la("sg", [P, 2, NT])
        hidf = la("hidf", [P, 2, NT])
        r_rows = la("r_rows", [P, 5, 3, N_EXPERTS])
        gate_t = la("gate_t", [N_EXPERTS, NT])
        r_hl = la("r_hl", [P, KD, P], F32R)
        two_idents = la("two_idents", [P, N_EXPERTS])
        late.close()
        r_turned = gate_bc[:, 0, :]
        r_stage = d_stage[:, 0, 0:KD * N_EXPERTS].rearrange("p (k n) -> p k n", k=KD)

        consts = sem("consts")
        vec_in, lam_in, router_in = sem("vec_in"), sem("lam_in"), sem("router_in")
        vec_turned, vec_ready, silu_ready = sem("vec_turned"), sem("vec_ready"), sem("silu_ready")
        lam_dots, lam_exps = sem("lam_dots"), sem("lam_exps")
        x_in = [sem(f"x_in{i}") for i in range(2)]
        xt_full, xt_taken, spilled, resid_in = sem("xt_full"), sem("xt_taken"), sem("spilled"), sem("resid_in")
        sq_ready, sq_used, log_ready, rstd_ready = sem("sq_ready"), sem("sq_used"), sem("log_ready"), sem("rstd_ready")
        padded, pad_cleared = sem("padded"), sem("pad_cleared")
        norm_ready, c_normed, c_squared, means_full = (
            sem("norm_ready"), sem("c_normed"), sem("c_squared"), sem("means_full"))
        hf_ready, h_hi_ready, h_lo_ready = sem("hf_ready"), sem("h_hi_ready"), sem("h_lo_ready")
        w_in_s = [sem(f"w_in{i}") for i in range(4)]
        w_hi_ready, w_lo_ready = sem("w_hi_ready"), sem("w_lo_ready")
        ada_rows, rows_copied, ada_full = sem("ada_rows"), sem("rows_copied"), sem("ada_full")
        proj_full, proj_taken, resid_ready = sem("proj_full"), sem("proj_taken"), sem("resid_ready")
        qk_full = [sem(f"qk_full{i}") for i in range(4)]
        qk_free = [sem(f"qk_free{i}") for i in range(4)]
        tr_full = [sem(f"tr_full{i}") for i in range(2)]
        tr_free = [sem(f"tr_free{i}") for i in range(2)]
        o_full, o_free = sem("o_full"), sem("o_free")
        cache_in, v_cache_in = sem("cache_in"), sem("v_cache_in")
        k_rows_out = [sem(f"k_rows_out{i}") for i in range(2)]
        rows_out = sem("rows_out")
        score_ready, picked = sem("score_ready"), sem("picked")
        bias_ready, exp_ready, p_ready = sem("bias_ready"), sem("exp_ready"), sem("p_ready")
        l_ready, capped, sp_ready, run_ready = sem("l_ready"), sem("capped"), sem("sp_ready"), sem("run_ready")
        av_done = sem("av_done")
        dve_step, act_step = sem("dve_step"), sem("act_step")
        r_full, r_taken, gates_ready, gates_turned, gates_copied, gates_out = (
            sem("r_full"), sem("r_taken"), sem("gates_ready"), sem("gates_turned"), sem("gates_copied"), sem("gates_out"))
        gu_in = [sem(f"gu_in{i}") for i in range(2)]
        d_in = sem("d_in")
        g_in = [sem(f"g_in{i}") for i in range(GROUP)]
        gu_hi_ready, gu_lo_ready, d_hi_ready, d_lo_ready = (
            sem("gu_hi_ready"), sem("gu_lo_ready"), sem("d_hi_ready"), sem("d_lo_ready"))
        au_full, sg_ready, gated, hid_ready = sem("au_full"), sem("sg_ready"), sem("gated"), sem("hid_ready")
        hid_hi_ready, hid_lo_ready, down_full, y_added = (
            sem("hid_hi_ready"), sem("hid_lo_ready"), sem("down_full"), sem("y_added"))
        fin_ready, scaled, row_root_ready, row_rstd_ready = (
            sem("fin_ready"), sem("scaled"), sem("row_root_ready"), sem("row_rstd_ready"))
        y_full, y_taken, y_out = sem("y_full"), [sem(f"y_taken{i}") for i in range(2)], sem("y_out")

        qk = Ring(4, qk_full, qk_free)
        tr = Ring(2, tr_full, tr_free)
        o_uses, n_o = {}, 0
        for n in range(4):
            tr.use(("ada", n), fills=0)
        for step in SCHEDULE:
            kind = step[0]
            if kind == "score":
                qk.use(step, among=3)
            elif kind == "qk":
                for m in range(2 if step[1] == "c" else 1):
                    qk.use(step[1:] + (m,), among=4 if step[1] == "c" else 3)
            elif kind == "z":
                qk.use(step[1:], fills=2)
            elif kind == "rows":
                tr.use(step + (0,))
                tr.use(step + (1,))
            elif kind in ("pt", "cache", "means"):
                tr.use(step)
            elif kind == "ada":
                tr.use(step, fills=0)
            if kind == "pv" or (kind == "av" and step[3] == 0):
                o_uses[step] = n_o
                n_o += 1
        score_bank, tr_bank, o_bank = bank[2:5] + bank[1:2], bank[5:7], bank[7]

        assert [step[1] for step in SCHEDULE if step[0] == "proj"] == list(range(N_IN))
        N_SPLIT = N_IN + KD
        stage_order = [("ada", n) for n in range(16)] + [("w", 0)]
        for step in SCHEDULE:
            if step[0] == "ada":
                stage_order += [("ada", 4 * step[1] + i) for i in range(4)]
            if step[0] == "proj":
                stage_order.append(("w", step[1] + 1))
        stage_order += [("w", N_IN + i) for i in range(1, KD)]
        stage_no = {item: i for i, item in enumerate(stage_order)}
        stage_value, _v = {}, [0] * 4
        for i, item in enumerate(stage_order):
            _v[i % 4] += 32 if item == ("w", 0) else 16
            stage_value[item] = _v[i % 4]

        def wait_stage(eng, item):
            eng.wait_ge(w_in_s[stage_no[item] % 4], stage_value[item])

        def staged(item):
            return w_stage[:, stage_no[item] % 4]

        def index_of(kinds):
            return {st: i for i, st in enumerate(x for x in SCHEDULE if x[0] in kinds)}

        score_no = index_of(("score",))
        unit_no = {st[1:]: i for st, i in index_of(("qk",)).items()}
        stick_no = {st[1:]: i for st, i in index_of(("z",)).items()}
        unit_key = {i: k for k, i in unit_no.items()}
        stick_key = {i: k for k, i in stick_no.items()}
        rows_steps = [x for x in SCHEDULE if x[0] == "rows"]
        k_fill = {}
        for st in rows_steps:
            if TILES[st[1]][0][0] == "k":
                k_fill[st] = len(k_fill)
        map_no, n_maps = {}, 0
        for st in SCHEDULE:
            if st[0] == "qk":
                for m in range(2 if st[1] == "c" else 1):
                    map_no[st[1:] + (m,)] = n_maps
                    n_maps += 1

        def feat(slot):
            return resid[:, slot, :] if slot < 8 else feat2[:, slot - 8, :]

        def v_of(group):
            return v_rows[1 if group in ("b", "s") else 0]

        def cache_slot(group):
            return {"i": 0, "a": 1, "b": 0, "c": 1}[group]

        def last_step(pred):
            return [x for x in SCHEDULE if pred(x)][-1]

        last_score = last_step(lambda x: x[0] == "score")
        last_a_pv = last_step(lambda x: x[0] == "pv" and x[1] == "a")

        last_a_qk = last_step(lambda x: x[0] == "qk" and x[1] == "a")

        def cache_blocks(g, part):
            nf = {"i": 1, "a": 2, "b": 3, "c": 3}[g]
            return [(f, t) for f in range(nf) for t in range(2)][4 * part:4 * part + 4]

        def stick_rows(key):
            return N_SAMPLE if key[0] == "s" and key[2] == 2 else P

        def stick_width(key):
            return H_B // 2 * N_SAMPLE if key[0] == "s" else N_PROMPT - P * key[2]

        def softplus(key):
            u, w = stick_no[key], stick_width(key)
            if key[0] == "b":
                return sp_buf[:, u % 3, 0:w]
            c = w * (u - 4 * H_B)
            return sp_buf[:, :, :].rearrange("p s c -> p (s c)")[:, c:c + w]

        row_sources = [st[1] for st in rows_steps if TILES[st[1]][0][0] in "vw"]

        def pad_rows(key, m):
            w = QK_C if key[0] == "c" else HD
            r0 = HD * (key[1] % 2) + w * m
            return slice(r0, r0 + w)

        def pad_slot(key, m):
            g, h, t = key
            if g == "b":
                return k_pad[:, 2 * (h % 2) + stick_no[key] % 2, :]
            u = unit_no[key]
            return q_pad[:, 2 * (2 * (h % 2) + m) + (u // 2 if g == "a" else u) % 2, :]

        pad_no, pad_before, at = {}, {}, {}
        for st in SCHEDULE:
            if st[0] == "pad":
                g, h = st[1:3]
                u = stick_no[st[1:]] if g == "b" else unit_no[st[1:]]
                for m in range(2 if g == "c" else 1):
                    slot = (g, h % 2, m, (u // 2 if g == "a" else u) % 2)
                    n = len(pad_no)
                    pad_no[st[1:] + (m,)] = n
                    if slot in at:
                        pad_before[n] = at[slot]
                    at[slot] = st[1:] if g == "b" else st[1:] + (m,)

        def split_low(eng, e, n):
            eng.wait_ge(w_hi_ready, n + 1)
            e.tensor_tensor(w_lo[:, n % 2], staged(("w", n)), w_hi[:, n % 2].bitcast(F32), ALU.subtract)\
                .then_inc(w_lo_ready, 1)

        Y_PARTS = [(0, 0), (1, 0), (2, 0), (3, 0), (0, 1), (1, 1), (2, 1), (3, 1), (4, 0), (4, 1)]
        Y_BANKS = [bank[i] for i in (0, 1, 2, 3, 5, 6, 7)]

        def wait_y_taken(eng, i):
            eng.wait_ge(y_taken[i % 2], i // 2 + 1)

        def y_rows(t):
            return gu_stage[:, t % 2, t // 2].rearrange("p k f -> p (k f)") if t < 4 else d_stage[:, 0, :]

        def y_part(i):
            t, c = Y_PARTS[i]
            n = tokens(t)[1]
            return y_rows(t)[0:n, 512 * c:512 * c + 512], Y_BANKS[i % 7][0:n, :], row_rstd[0:n, t:t + 1]

        def constants(pool, first):
            g = nc.gpsimd
            n = 0 if first else 2

            def made(ins):
                nonlocal n
                n += 1
                ins.then_inc(consts, 1)
                pool.wait_ge(consts, n)

            def masked(t, fill0, pattern, cm, op, fill):
                made(g.memset(t, fill0))
                made(g.affine_select(out=t, in_=t, compare_op=op, fill=fill, base=0, pattern=pattern,
                                     channel_multiplier=cm))

            if first:
                masked(ident[:, :], 0.0, [[-1, P]], 1, ALU.not_equal, 1.0)
                return
            made(g.memset(eps_col[:, :], EPS))
            made(g.memset(ones[:, :], 1.0))
            made(g.memset(neg_ones[:, :], -1.0))
            masked(neg_tri[:, :], -1.0, [[-1, P]], 1, ALU.is_ge, 0.0)
            masked(diag_neg[:, :], 0.0, [[1, P]], -1, ALU.is_gt, NEG)
            masked(diag_01[:, :], 1.0, [[1, P]], -1, ALU.is_gt, 0.0)
            masked(diag_neg_s[:, :, :], 0.0, [[0, H_B // 2], [1, N_SAMPLE]], -1, ALU.is_gt, NEG)
            masked(diag_01_s[:, :, :], 1.0, [[0, H_B // 2], [1, N_SAMPLE]], -1, ALU.is_gt, 0.0)
            made(g.memset(two_heads[:, :], 0.0))
            made(g.memset(two_heads[0:HD, 0:HD], 1.0))
            made(g.memset(two_heads[HD:P, HD:P], 1.0))
            made(g.iota(dist[:, :], pattern=[[-1, 512]], base=DIST0, channel_multiplier=1,
                        allow_small_or_imprecise_dtypes=True))

        N_CONSTS = 6 * 2 + 2 + 3 + 2

        block = ctx.enter_context(nc.Block())

        @block.sync
        def _(sp):
            w_ada = io["w_ada"][0].rearrange("(k p) e -> p k e", p=P)
            w_in = io["w_in"][0].rearrange("(k p) e -> p k e", p=P)
            w_out = io["w_out"][0].rearrange("(k p) e -> p k e", p=P)
            for i, item in enumerate(stage_order):
                if i >= 4:
                    before, n_before = stage_order[i - 4]
                    sp.wait_ge(w_lo_ready if before == "w" else ada_rows, n_before + 1)
                dst = w_stage[:, i % 4]
                s = w_in_s[i % 4]
                kind, n = item
                if kind == "ada":
                    sp.dma_start(dst, w_ada[:, :, P * n:P * n + P]).then_inc(s, 16)
                elif n >= N_IN:
                    e = n - N_IN
                    sp.dma_start(dst, w_out[:, :, P * e:P * e + P]).then_inc(s, 16)
                elif n == 0:
                    c = COL["ki"]
                    for j in range(2):
                        sp.dma_start(dst[:, :, HD * j:HD * j + HD], w_in[:, :, c:c + HD]).then_inc(s, 16)
                else:
                    name, j = TILES[n]
                    c = COL[name] + P * j
                    sp.dma_start(dst, w_in[:, :, c:c + P]).then_inc(s, 16)

            gate_up = [io["w_e_gate"][0].rearrange("e (k p) f -> e p k f", p=P),
                       io["w_e_up"][0].rearrange("e (k p) f -> e p k f", p=P)]
            down = io["w_e_down"][0].rearrange("(g e) f d -> g f e d", e=GROUP)
            sp.wait_ge(h_hi_ready, 2 * KD)
            sp.wait_ge(h_lo_ready, 2 * KD)
            for m, name in enumerate(("w_s_gate", "w_s_up")):
                sp.dma_start(gu_stage[:, 0, m], io[name][0].rearrange("(k p) f -> p k f", p=P)).then_inc(gu_in[0], 16)

            def load_gate_up(g, e):
                if isinstance(g, int) and g == 0 and e == 0:
                    pass
                else:
                    sp.wait_ge(gu_lo_ready, g * GROUP + e)
                for m in range(2):
                    sp.dma_start(gu_stage[:, (1 + e) % 2, m], gate_up[m][g * GROUP + e])\
                      .then_inc(gu_in[(1 + e) % 2], 16)

            def load_down(g):
                sp.wait_ge(d_lo_ready, g * KD + KD)
                sp.dma_start(d_stage[:, :, :], down[g]).then_inc(d_in, 16)

            load_gate_up(0, 0)
            sp.wait_ge(resid_ready, 2 * KD)
            sp.wait_ge(sq_used, 2 * KD)
            sp.dma_start(r_stage, io["w_router"][0].rearrange("(k p) n -> p k n", p=P)).then_inc(router_in, 16)
            sp.dma_start(b_rows[:, :], io["b_router"].broadcast_to([P, N_EXPERTS])).then_inc(router_in, 16)
            sp.wait_ge(r_taken, 2)
            sp.dma_start(d_stage[:, 0, :], io["w_s_down"][0]).then_inc(d_in, 16)
            load_gate_up(0, 1)
            load_down(0)
            load_gate_up(0, 2)
            load_gate_up(0, 3)
            with sp.Fori(1, N_GROUPS) as g:
                load_gate_up(g, 0)
                load_gate_up(g, 1)
                load_down(g)
                load_gate_up(g, 2)
                load_gate_up(g, 3)

            y_p = io["y_prompt"].rearrange("b (t p) d -> (b t) p d", p=P)
            for t in range(5):
                for c in range(2):
                    wait_y_taken(sp, Y_PARTS.index((t, c)))
                n = tokens(t)[1]
                dst = y_p[t] if t < 4 else io["y_sample"][0]
                sp.dma_start(dst, y_rows(t)[0:n, :]).then_inc(y_out, 16)
            sp.wait_ge(y_out, 5 * 16)

        @block.gpsimd
        def _(pool):
            for name, r0, n in (("b_ada", 0, 48), ("g_final", 48, 8), ("c_prompt", 56, 8), ("c_sample", 64, 8)):
                a = io[name] if name == "g_final" else io[name][0]
                pool.dma_start(vec_rows[r0:r0 + n, :], a.rearrange("(r c) -> r c", c=P)).then_inc(vec_in, 16)
            for j in range(2):
                pool.dma_start(vec_rows[72:73, HD * j:HD * j + HD], io["subln_diff"]).then_inc(vec_in, 16)
            xp = io["x_prompt"].rearrange("b (t p) d -> (b t) p d", p=P)
            for t in range(5):
                if t >= 2:
                    pool.wait_ge(xt_taken, 2 * (t - 1))
                n = tokens(t)[1]
                pool.dma_start(x_rows[0:n, t % 2, :], xp[t] if t < 4 else io["x_sample"][0]).then_inc(x_in[t % 2], 16)
                if t == 1:
                    constants(pool, True)
            constants(pool, False)
            pool.dma_start(lam_rows[:, :], io["lam_diff"].rearrange("l a b -> l (a b)").broadcast_to([P, 4 * QK_C]))\
                .then_inc(lam_in, 16)
            pool.wait_ge(xt_taken, 10)
            pool.dma_start(x_spill, o_t[:, :, :]).then_inc(spilled, 16)

            caches = {"i": io["cache_sparse_kidx"][0, 0], "a": io["cache_sparse_kv"][0, 0],
                      "b": io["cache_stick_kv"][0, 0], "c": io["cache_diff_kv"][0, 0]}
            width = {"a": H_A * HD, "b": H_B * HD, "c": H_C * HD}

            def load_cache(g):
                if g == "i":
                    src = caches[g].rearrange("(t p) c -> p t c", p=P)
                    for j in range(2):
                        pool.dma_start(cache_rows[:, :, HD * j:HD * j + HD], src).then_inc(cache_in, 16)
                    return
                src = caches[g].rearrange("(t p) kv h d -> p t kv (h d)", p=P)
                before = {"a": ("cache", "i", 0), "b": ("cache", "a", 0), "c": ("cache", "b", 1)}[g]
                tr.wait_full(pool, before)
                pool.dma_start(cache_rows[:, :, 0:width[g]], src[:, :, 0, :]).then_inc(cache_in, 16)
                if g == "c":
                    pool.wait_ge(o_full, unit_no[last_a_pv[1:]] + 1)
                pool.dma_start(v_of(g)[:, 4:6, 0:width[g]], src[:, :, 1, :]).then_inc(v_cache_in, 16)

            out_p = {"ki": io["ki_p"], "ka": io["kv_a_p"][:, 0], "va": io["kv_a_p"][:, 1],
                     "kb": io["kv_b_p"][:, 0], "vb": io["kv_b_p"][:, 1],
                     "kc": io["kv_c_p"][:, 0], "vc": io["kv_c_p"][:, 1]}
            out_s = {"ki": io["ki_s"], "ka": io["kv_a_s"][:, 0], "va": io["kv_a_s"][:, 1],
                     "kb": io["kv_b_s"][:, 0], "vb": io["kv_b_s"][:, 1],
                     "kc": io["kv_c_s"][:, 0], "vc": io["kv_c_s"][:, 1]}

            def store_rows(step):
                name, j = TILES[step[1]]
                if name == "wi":
                    return
                w = HD if name == "ki" else P
                for half in range(2):
                    tr.wait_taken(pool, step + (half,))
                if name[0] == "k":
                    n = k_fill[step]
                    src_p, src_s = k_rows[:, n % 2, 0:4, 0:w], k_rows[0:N_SAMPLE, n % 2, 4, 0:w]
                    s = k_rows_out[n % 2]
                else:
                    v = v_of(name[1])
                    src_p, src_s = v[:, 0:4, P * j:P * j + w], v[0:N_SAMPLE, 6, P * j:P * j + w]
                    s = rows_out
                pool.dma_start(out_p[name].rearrange("(t p) c -> p t c", p=P)[:, :, P * j:P * j + w], src_p)\
                    .then_inc(s, 16)
                pool.dma_start(out_s[name][:, P * j:P * j + w], src_s).then_inc(s, 16)

            last_op = []

            def after_last(sem_, value):
                if last_op:
                    pool.wait_ge(*last_op.pop())
                last_op.append((sem_, value))

            def table(h):
                if h >= 2:
                    for t in range(5):
                        qk.wait_taken(pool, ("c", h - 2, t, 1))
                after_last(bias_ready, h + 1)
                nc.gpsimd.tensor_scalar(bias[:, h % 2, :], dist[:, :], -SLOPE_C[h] / SCALE_C, None, ALU.mult)\
                    .then_inc(bias_ready, 1)

            def pad(key):
                g, h, t = key
                if key in (("a", 0, 1), ("c", 0, 0)):
                    if g == "c":
                        pool.wait_ge(av_done, len(stick_no))
                    pool.wait_ge(proj_taken, 2 * (12 if g == "a" else N_IN))
                    after_last(pad_cleared, 1 if g == "a" else 3)
                    nc.gpsimd.memset(q_pad[:, :, :], 0.0).then_inc(pad_cleared, 1)
                    pool.wait_ge(pad_cleared, 1 if g == "a" else 3)
                if key == ("b", 0, 3):
                    for u in range(H_A):
                        qk.wait_taken(pool, ("a", u, 0, 0))
                    after_last(pad_cleared, 2)
                    nc.gpsimd.memset(k_pad[:, :, :], 0.0).then_inc(pad_cleared, 1)
                    pool.wait_ge(pad_cleared, 2)
                for m in range(2 if g == "c" else 1):
                    n = pad_no[key + (m,)]
                    if n in pad_before:
                        qk.wait_full(pool, pad_before[n])
                    r, c0, cols = pad_rows(key, m), P * t, P
                    if g != "b":
                        c0, cols = tokens(t)
                    src = feat(SLOT[("k" if g == "b" else "q") + g] + h // 2)
                    after_last(padded, n + 1)
                    nc.gpsimd.tensor_copy(pad_slot(key, m)[r, 0:cols], src[r, c0:c0 + cols]).then_inc(padded, 1)

            load_cache("i")
            for step in SCHEDULE:
                if step[0] == "split_o" and step[1] < MIX["c"]:
                    k = step[1]
                    pool.wait_ge(h_hi_ready, KD + k + 1)
                    after_last(h_lo_ready, KD + k + 1)
                    nc.gpsimd.tensor_tensor(h_lo[:, k, :], o_t[:, k, :], h_hi[:, k, :].bitcast(F32), ALU.subtract)\
                        .then_inc(h_lo_ready, 1)
                if step[0] == "split_w":
                    after_last(w_lo_ready, step[1] + 1)
                    split_low(pool, nc.gpsimd, step[1])
                if step[0] == "proj":
                    if step[1] == 0:
                        pool.wait_ge(w_lo_ready, 1)
                    after_last(w_lo_ready, step[1] + 2)
                    split_low(pool, nc.gpsimd, step[1] + 1)
                if step[0] == "rows":
                    store_rows(step)
                if step[0] == "pad":
                    pad(step[1:])
                if step == ("score", 1, 0):
                    load_cache("a")
                if step == ("cache", "a", 0):
                    load_cache("b")
                if step == ("cache", "c", 0):
                    load_cache("c")
                if step == ("pad", "c", 0, 0):
                    qk.wait_full(pool, ("b", H_B - 1, 0))
                    table(0)
                if step[0:2] == ("max", "c") and step[3] == 2 and step[2] < H_C - 1:
                    table(step[2] + 1)
            for m in range(2):
                qk.wait_full(pool, ("c", H_C - 1, 4, m))
            pool.wait_ge(spilled, 16)
            pool.dma_start(resid[:, :, :], x_spill).then_inc(resid_in, 16)
            for i in range(2):
                pool.wait_ge(k_rows_out[i], 32 * len([n for n in k_fill.values() if n % 2 == i]))
            pool.wait_ge(rows_out, 32 * 8)

            pool.wait_ge(gated, 2 * GROUP)
            pool.dma_start(gate_rows, gate_t[:, :]).then_inc(gates_out, 16)
            pool.wait_ge(gates_out, 16)
            with pool.Fori(0, N_GROUPS) as g:
                for e in range(GROUP):
                    pool.wait_ge(gated, (g * GROUP + e + 1) * 2)
                    pool.dma_start(gate_bc[:, e, :], gate_rows[bass.ds(g * GROUP + e, 1), :].broadcast_to([P, NT]))\
                        .then_inc(g_in[e], 16)

        @block.scalar
        def _(act):
            n_step = 0

            def chain(ins):
                nonlocal n_step
                n_step += 1
                ins.then_inc(act_step, 1)
                act.wait_ge(act_step, n_step)

            def square(r, k, dst, src):
                if k >= 2:
                    act.wait_ge(sq_used, KD * r + k - 1)
                nc.scalar.activation(dst[:, k % 2, :], src, ACT.Square).then_inc(sq_ready, 1)

            def inverse_root(logs):
                act.wait_ge(log_ready, logs)
                nc.scalar.activation(rstd[:, :], log_ms[:, :], ACT.Exp, scale=-0.5).then_inc(rstd_ready, 1)

            def root(r):
                act.wait_ge(means_full, (1, 5)[r])
                for b in range(2):
                    nc.scalar.activation(log_ms[:, HALF * b:HALF * b + HALF], bank[b][:, 0:HALF], ACT.Ln,
                                         scale=1.0 / D, bias=eps_col[:, 0:1]).then_inc(log_ready, 1)
                inverse_root((2, 7)[r])

            def split_high(n):
                wait_stage(act, ("w", n))
                if n >= 2:
                    act.wait_ge(proj_full, 2 * (n - 1))
                nc.scalar.copy(w_hi[:, n % 2], staged(("w", n))).then_inc(w_hi_ready, 1)

            def modulated(dst, c, normed, affine, tiles=range(KD)):
                for k in tiles:
                    w = dst[:, k % 2, :]
                    act.wait_ge(norm_ready, normed + k + 1)
                    for b, (a, z) in enumerate(((0, N_PROMPT), (N_PROMPT, NT))):
                        nc.scalar.activation(w[:, a:z], w[:, a:z], ACT.Identity, scale=mod[:, c + KD + k, b:b + 1],
                                             bias=mod[:, c + k, b:b + 1]).then_inc(hf_ready, 1)
                    act.wait_ge(hf_ready, affine + 2 * k + 2)
                    nc.scalar.copy(h_hi[:, k, :], w).then_inc(h_hi_ready, 1)

            act.wait_ge(vec_ready, 1)
            nc.scalar.activation(silu_c[:, :, :].rearrange("p k b -> p b k"),
                                 vec[:, 56:72].rearrange("p (b k) -> p b k", b=2), ACT.Silu).then_inc(silu_ready, 1)

            act.wait_ge(xt_taken, 10)
            for k in range(KD):
                square(0, k, sq, o_t[:, k, :])
            act.preload_act_table_set("natural_log_exp_and_others")
            act.wait_ge(consts, N_CONSTS)
            root(0)
            modulated(hf, 0, 0, 0, range(0, 4))
            split_high(0)
            modulated(hf, 0, 0, 0, range(4, KD - 2))
            split_high(1)
            modulated(hf, 0, 0, 0, range(KD - 2, KD))

            def evacuate_projection(n):
                name, j = TILES[n]
                for b in range(2):
                    act.wait_ge(proj_full, 2 * n + b + 1)
                    if name in ("wi", "va", "vb", "vc"):
                        m = row_sources.index(n)
                        dst = v_t[:, m % 2, :]
                        if b == 0 and m >= 2:
                            for half in range(2):
                                tr.wait_full(act, ("rows", row_sources[m - 2], half))
                    else:
                        dst = feat(SLOT[name] + j)
                        if b == 0 and name in ("qc", "kc"):
                            qk.wait_full(act, last_score)
                    nc.scalar.activation(dst[:, HALF * b:HALF * b + HALF], bank[b][:, 0:HALF], ACT.Copy,
                                         scale=SCALE_A if name == "qb" else 1.0).then_inc(proj_taken, 1)

            def evacuate_rows(step):
                name, j = TILES[step[1]]
                key = [step + (i,) for i in range(2)]
                src = [tr_bank[tr.bank(k)] for k in key]
                if name == "wi":
                    w, scale = N_IDX, N_IDX ** -0.5
                    dst = [wi_rows[:, 0:4, :], wi_rows[0:N_SAMPLE, 4, :]]
                elif name[0] == "k":
                    w, scale = HD if name == "ki" else P, 1.0
                    n = k_fill[step]
                    if n >= 2:
                        act.wait_ge(k_rows_out[n % 2], 32 * (n // 2))
                    dst = [k_rows[:, n % 2, 0:4, 0:w], k_rows[0:N_SAMPLE, n % 2, 4, 0:w]]
                else:
                    w, scale = P, 1.0
                    v = v_of(name[1])
                    if name == "vc" and j == 0:
                        act.wait_ge(o_full, unit_no[last_a_pv[1:]] + 1)
                        act.wait_ge(rows_out, 32 * 5)
                    dst = [v[:, 0:4, P * j:P * j + P], v[0:N_SAMPLE, 6, P * j:P * j + P]]
                tr.wait_full(act, key[0])
                nc.scalar.activation(dst[0], src[0][:, 0:4 * w].rearrange("p (t c) -> p t c", t=4), ACT.Copy,
                                     scale=scale).then_inc(tr_free[tr.bank(key[0])], 1)
                tr.wait_full(act, key[1])
                nc.scalar.activation(dst[1], src[1][0:N_SAMPLE, 0:w], ACT.Copy, scale=scale)\
                    .then_inc(tr_free[tr.bank(key[1])], 1)

            for step in SCHEDULE:
                kind, key = step[0], step[1:]
                if kind == "proj":
                    if step[1]:
                        split_high(step[1] + 1)
                    evacuate_projection(step[1])
                    if step[1] == 1:
                        act.wait_ge(lam_dots, 2)
                        nc.scalar.activation(lam_exp[:, :], lam_dot[:, :], ACT.Exp).then_inc(lam_exps, 1)
                elif kind == "split_w":
                    split_high(step[1])
                elif kind == "rows":
                    evacuate_rows(step)
                elif kind == "cache":
                    g, part = key
                    tr.wait_full(act, step)
                    blocks = cache_blocks(g, part)
                    f0 = blocks[0][0]
                    nf = len(blocks) // 2
                    if part == 0 and g == "b":
                        qk.wait_full(act, last_score)
                    if part == 0 and g == "c":
                        qk.wait_full(act, last_a_qk[1:] + (0,))
                    nc.scalar.copy(cache_t[:, cache_slot(g), f0:f0 + nf, :],
                                   tr_bank[tr.bank(step)][:, 0:256 * nf].rearrange("p (f c) -> p f c", f=nf))\
                        .then_inc(tr_free[tr.bank(step)], 1)
                elif kind == "score":
                    t, h = key
                    n, m = keys(t), score_no[step]
                    rows = tokens(t)[1]
                    qk.wait_full(act, step)
                    if m >= 2:
                        act.wait_ge(score_ready, m - 1)
                    qk.take(nc.scalar.activation(bias[0:rows, m % 2, 0:n], score_bank[qk.bank(step)][0:rows, 0:n],
                                                 ACT.Relu, scale=HD ** -0.5), step)
                elif kind == "max":
                    g, h, t = key
                    rows, n, u = tokens(t)[1], keys(t), unit_no[key]
                    for m in range(2 if g == "c" else 1):
                        qk.wait_taken(act, key + (m,))
                        w = p_work[0:rows, 2 * (u % 3) + m, 0:n]
                        nc.scalar.activation(w, w, ACT.Exp, scale=-1.0, bias=n_max[0:rows, u % 2, m:m + 1],
                                             accum_out=p_sum[0:rows, u % 2, m:m + 1]).then_inc(exp_ready, 1)
                elif kind == "pt":
                    g, h, t = key
                    rows, n, u = tokens(t)[1], keys(t), unit_no[key]
                    tr.wait_full(act, step)
                    if u >= 2:
                        act.wait_ge(o_full, u - 1)
                    if key == ("c", 0, 0):
                        act.wait_ge(sp_ready, len(stick_no))
                    src = tr_bank[tr.bank(step)]
                    full = n // P
                    ins = nc.scalar.copy(p_t[:, u % 2, 0:full, 0:rows],
                                         src[:, 0:full * rows].rearrange("p (j q) -> p j q", j=full))
                    if n % P:
                        chain(ins)
                        ins = nc.scalar.copy(p_t[0:n % P, u % 2, full, 0:rows],
                                             src[0:n % P, full * rows:(full + 1) * rows])
                    ins.then_inc(tr_free[tr.bank(step)], 1)
                elif kind == "pv" and key[0] == "c":
                    g, h, t = key
                    c0, rows = tokens(t)
                    r = slice(HD * (h % 2), HD * (h % 2) + HD)
                    act.wait_ge(o_full, unit_no[key] + 1)
                    nc.scalar.copy(o_t[r, MIX[g] + h // 2, c0:c0 + rows], o_bank[r, 0:rows]).then_inc(o_free, 1)
                elif kind == "square":
                    if key[0] == 0:
                        act.wait_ge(sp_ready, len(stick_no))
                        qk.wait_full(act, stick_key[len(stick_no) - 1], 2)
                    else:
                        tr.wait_full(act, ("means", key[0] - 1))
                    act.wait_ge(o_free, o_uses[("pv", "c", 2 * key[0] + 1, 4)] + 1)
                    nc.scalar.activation(c_sq, o_t[:, MIX["c"] + key[0], :], ACT.Square).then_inc(c_squared, 1)
                elif kind == "root":
                    i = key[0]
                    act.wait_ge(rstd_ready, 1 + i)
                    act.wait_ge(means_full, 2 + i)
                    step = ("means", i)
                    nc.scalar.activation(log_ms[:, 0:N_PROMPT], bank[0][:, 0:N_PROMPT], ACT.Ln, scale=1.0 / HD,
                                         bias=eps_col[:, 0:1]).then_inc(log_ready, 1)
                    tr.wait_full(act, step)
                    tr.take(nc.scalar.activation(log_ms[:, N_PROMPT:NT], tr_bank[tr.bank(step)][:, 0:N_SAMPLE], ACT.Ln,
                                                 scale=1.0 / HD, bias=eps_col[:, 0:1]), step)
                    tr.wait_taken(act, step)
                    if i:
                        act.wait_ge(c_normed, i)
                    inverse_root(3 + i)
                elif kind == "split_o":
                    k = key[0]
                    if k == 0:
                        act.wait_ge(proj_full, 2 * N_IN)
                        act.wait_ge(o_free, o_uses[("pv", "c", 0, 0)])
                    if k >= MIX["c"]:
                        act.wait_ge(c_normed, k - MIX["c"] + 1)
                    nc.scalar.copy(h_hi[:, k, :], o_t[:, k, :]).then_inc(h_hi_ready, 1)
                elif kind == "z":
                    rows, w, u = stick_rows(key), stick_width(key), stick_no[key]
                    act.wait_ge(capped, u + 1)
                    l = l_buf[0:rows, u % 2, 0:w]
                    chain(nc.scalar.activation(l, l, ACT.Exp))
                    nc.scalar.activation(l, l, ACT.Ln, bias=1.0).then_inc(l_ready, 1)
                elif kind == "acc":
                    rows, w, u = stick_rows(key), stick_width(key), stick_no[key]
                    qk.wait_full(act, key, 2)
                    if u >= 2:
                        act.wait_ge(av_done, u - 1)
                    b = qk.bank(key)
                    qk.take(nc.scalar.activation(a_t[0:rows, u % 2, 0:w], score_bank[b][0:rows, 0:w], ACT.Exp), key)

            def gu_high(s, loads):
                act.wait_ge(gu_in[s], loads)
                nc.scalar.copy(gu_hi[:, s], gu_stage[:, s]).then_inc(gu_hi_ready, 1)

            act.wait_ge(rows_out, 32 * 8)
            for e in range(KD):
                if e + 2 < KD:
                    split_high(N_IN + e + 2)
                elif e + 2 == KD:
                    gu_high(0, 32)
                act.wait_ge(resid_ready, 2 * e + 2)
                square(1, e, sq, resid[:, e, :])
            root(1)
            modulated(hidf, 3 * KD, KD, 2 * KD)
            act.wait_ge(router_in, 32)
            nc.scalar.copy(r_hl[:, :, 0:N_EXPERTS], r_stage).then_inc(r_taken, 1)

            def down_high(n_d, d, q, n_e):
                if d == 0:
                    act.wait_ge(d_in, 16 * q + 16)
                if not (isinstance(q, int) and q == 0 and d < 2):
                    act.wait_ge(down_full, n_d * 2 - 2)
                nc.scalar.copy(d_hi[:, d % 2, 0:n_e, :], d_stage[:, 0:n_e, P * d:P * d + P]).then_inc(d_hi_ready, 1)

            def silu(n, slot):
                for b in range(2):
                    act.wait_ge(au_full, n * 4 + b + 1)
                    nc.scalar.activation(sg[:, slot, HALF * b:HALF * b + HALF], bank[b][:, 0:HALF], ACT.Silu)\
                        .then_inc(sg_ready, 1)

            def hid_high(n, slot, e):
                for b in range(2):
                    act.wait_ge(hid_ready, n * 2 + b + 1)
                    nc.scalar.copy(hid_hi[:, e, HALF * b:HALF * b + HALF], hidf[:, slot, HALF * b:HALF * b + HALF])\
                        .then_inc(hid_hi_ready, 1)

            silu(0, 0)
            gu_high(1, 32)
            hid_high(0, 0, 0)
            down_high(0, 0, 0, 1)
            down_high(1, 1, 0, 1)
            for b in range(2):
                act.wait_ge(r_full, b + 1)
                nc.scalar.copy(r_turned[:, HALF * b:HALF * b + HALF], bank[4 + b][:, 0:HALF]).then_inc(r_taken, 1)
            act.wait_ge(r_full, 3)
            nc.scalar.activation(r_rows[:, :, 0, :], bank[7][:, 0:5 * N_EXPERTS].rearrange("p (t n) -> p t n", t=5),
                                 ACT.Sigmoid).then_inc(r_taken, 1)
            for d in range(2, KD):
                down_high(d, d, 0, 1)

            def group(g, last):
                for e in range(GROUP):
                    n = g * GROUP + (1 + e)
                    slot = (1 + e) % 2
                    if e < GROUP - 1:
                        act.wait_ge(au_full, n * 4)
                        gu_high((2 + e) % 2, (g * 2 + 1 + (2 + e) // 2) * 32)
                    else:
                        down_high(g * KD + KD, 0, g + 1, GROUP)
                        down_high(g * KD + KD + 1, 1, g + 1, GROUP)
                    silu(n, slot)
                    if e == 0:
                        act.wait_ge(down_full, (g + 1) * 2 * KD)
                    hid_high(n, slot, e)
                for d in range(2, KD):
                    down_high(g * KD + (KD + d), d, g + 1, GROUP)
                    if d == 4 and not last:
                        act.wait_ge(au_full, (g * GROUP + GROUP) * 4)
                        gu_high(1, (g * 2 + 3) * 32)
                    if d >= 3 and last:
                        finished(d - 3)

            def finished(k):
                act.wait_ge(fin_ready, k + 1)
                square(2, k, sg, resid[:, k, :])
                nc.scalar.activation(y_acc[:, k, :], resid[:, k, :], ACT.Copy,
                                     scale=vec[:, 6 * KD + k:6 * KD + k + 1]).then_inc(scaled, 1)

            with act.Fori(0, N_GROUPS - 1) as g:
                group(g, False)
            group(N_GROUPS - 1, True)
            act.preload_act_table_set("sqrt_and_others")
            for k in range(KD - 3, KD):
                finished(k)

            act.wait_ge(means_full, 6)
            for rows, t in ((P, slice(0, 4)), (N_SAMPLE, slice(4, 5))):
                nc.scalar.activation(row_root[0:rows, t], bank[4][0:rows, t], ACT.Sqrt, scale=1.0 / D,
                                     bias=eps_col[0:rows, 0:1]).then_inc(row_root_ready, 1)
            act.wait_ge(row_rstd_ready, 2)
            for i in range(0, len(Y_PARTS), 2):
                rows, turned_y, inverse = y_part(i)
                act.wait_ge(y_full, i + 1)
                nc.scalar.activation(rows, turned_y, ACT.Copy, scale=inverse).then_inc(y_taken[0], 1)

        @block.tensor
        def _(pe):
            mm = nc.tensor.matmul

            def three(out, hi_w, lo_w, hi_x, lo_x, first, last):
                mm(out, hi_w, hi_x, start=first, stop=False)
                mm(out, hi_w, lo_x, start=False, stop=False)
                return mm(out, lo_w, hi_x, start=False, stop=last)

            def halves(b):
                return slice(HALF * b, HALF * b + HALF)

            def mean_square(r):
                pe.wait_ge(sq_used, KD * r + KD)
                for b in range(2):
                    ins = mm(bank[b][:, 0:HALF], ones[:, :], rstd[:, halves(b)], start=True, stop=True)
                ins.then_inc(means_full, 1)

            def modulation(n):
                step = ("ada", n)
                tr.wait_free(pe, step)
                for i in range(4):
                    item = ("ada", 4 * n + i)
                    wait_stage(pe, item)
                    for k in range(KD):
                        ins = mm(tr_bank[tr.bank(step)][0:2, P * i:P * i + P], silu_c[:, k, :], staged(item)[:, k, :],
                                 start=(k == 0), stop=(k == KD - 1))
                    ins.then_inc(ada_rows, 1)

            def turn_modulation(n):
                pe.wait_ge(rows_copied, n + 1)
                for j in range(4):
                    ins = nc.tensor.transpose(tr_bank[tr.bank(("ada", n))][:, 2 * j:2 * j + 2],
                                              mod_rows[:, P * j:P * j + P], ident[0:2, 0:2])
                ins.then_inc(ada_full, 1)

            def project(n):
                pe.wait_ge(w_lo_ready, n + 1)

                def product(b, k):
                    return three(bank[b][:, 0:HALF], w_hi[:, n % 2, k, :], w_lo[:, n % 2, k, :],
                                 h_hi[:, k, halves(b)], h_lo[:, k, halves(b)], k == 0, k == KD - 1)

                if n in (0, N_IN):
                    if n:
                        pe.wait_ge(log_ready, 5)
                        pe.wait_ge(qk_free[3], qk.uses[3])
                    for k in range(KD):
                        pe.wait_ge(h_lo_ready, (KD if n else 0) + k + 1)
                        for b in range(2):
                            ins = product(b, k)
                            if k == KD - 1:
                                ins.then_inc(proj_full, 1)
                    return
                for b in range(2):
                    if n < N_IN:
                        pe.wait_ge(proj_taken, 2 * (n - 1) + b + 1)
                    else:
                        pe.wait_ge(resid_ready, 2 * (n - 1 - N_IN) + b + 1)
                    for k in range(KD):
                        ins = product(b, k)
                    ins.then_inc(proj_full, 1)

            pe.wait_ge(consts, 2)
            pe.wait_ge(vec_in, 6 * 16)
            nc.tensor.transpose(bank[7][:, 0:73], vec_rows[0:73, :], ident[0:73, 0:73]).then_inc(vec_turned, 1)
            for kind, t in PROLOGUE:
                if kind == "ada":
                    if t == 0:
                        pe.wait_ge(silu_ready, 1)
                    modulation(t)
                if kind == "turn":
                    turn_modulation(t)
                if kind == "means":
                    pe.wait_ge(consts, N_CONSTS)
                    mean_square(0)
                if kind != "x":
                    continue
                c0, n = tokens(t)
                pe.wait_ge(x_in[t % 2], 16 * (t // 2 + 1))
                for c in range(2):
                    m = 2 * t + c
                    if m >= 3:
                        pe.wait_ge(xt_taken, m - 2)
                    for i in range(4):
                        k = 4 * c + i
                        ins = nc.tensor.transpose(bank[2 + m % 3][:, n * i:n * i + n], x_rows[0:n, t % 2, P * k:P * k + P],
                                                  ident[0:n, 0:n])
                    ins.then_inc(xt_full, 1)
            pe.wait_ge(xt_taken, 10)
            pe.wait_ge(log_ready, 2)

            def turn_rows(step):
                n = step[1]
                name, j = TILES[n]
                src = feat(SLOT[name] + j) if name[0] == "k" else v_t[:, row_sources.index(n) % 2, :]
                r = {"wi": N_IDX, "ki": HD}.get(name, P)
                pe.wait_ge(proj_taken, 2 * n + 2)
                tr.wait_free(pe, step + (0,))
                b = tr.bank(step + (0,))
                for t in range(4):
                    ins = nc.tensor.transpose(tr_bank[b][:, r * t:r * t + r], src[0:r, P * t:P * t + P], ident[0:r, 0:r])
                ins.then_inc(tr_full[b], 1)
                tr.wait_free(pe, step + (1,))
                b = tr.bank(step + (1,))
                nc.tensor.transpose(tr_bank[b][0:N_SAMPLE, 0:r], src[0:r, N_PROMPT:NT], ident[0:r, 0:r])\
                    .then_inc(tr_full[b], 1)

            cache_value = {"i": 32, "a": 48, "b": 64, "c": 80}

            def wait_cached(g):
                for part in range(2 if g in "bc" else 1):
                    tr.wait_taken(pe, ("cache", g, part))

            def wait_rows(name):
                for st in rows_steps:
                    if TILES[st[1]][0] == name:
                        for half in range(2):
                            tr.wait_taken(pe, st + (half,))

            def key_products(out, q, k_new, k_old, t):
                rows = tokens(t)[1]
                if t < 4:
                    return mm(out[:, 0:keys(t)], q, k_new[:, 0:keys(t)], start=True, stop=True)
                mm(out[0:rows, 0:PAST], q, k_old, start=True, stop=True)
                return mm(out[0:rows, PAST:N_KEYS_S], q, k_new[:, N_PROMPT:NT], start=True, stop=True)

            for step in SCHEDULE:
                kind, key = step[0], step[1:]
                if kind == "proj":
                    project(step[1])
                elif kind == "ada":
                    modulation(step[1])
                elif kind == "turn":
                    turn_modulation(step[1])
                elif kind == "rows":
                    turn_rows(step)
                elif kind == "cache":
                    g, part = key
                    pe.wait_ge(cache_in, cache_value[g])
                    tr.wait_free(pe, step)
                    b = tr.bank(step)
                    for i, (f, t) in enumerate(cache_blocks(g, part)):
                        ins = nc.tensor.transpose(tr_bank[b][:, P * i:P * i + P], cache_rows[:, t, P * f:P * f + P], ident[:, :])
                    ins.then_inc(tr_full[b], 1)
                elif kind == "score":
                    t, h = key
                    if t == 1 and h == 0:
                        pe.wait_ge(proj_taken, 2 * 6)
                        wait_cached("i")
                    r = slice(HD * (h % 2), HD * (h % 2) + HD)
                    qk.wait_free(pe, step)
                    b = qk.bank(step)
                    c0, rows = tokens(t)
                    key_products(score_bank[b], feat(SLOT["qi"] + h // 2)[r, c0:c0 + rows], feat(SLOT["ki"])[r, :],
                                 cache_t[r, cache_slot("i"), 0, :], t).then_inc(qk_full[b], 1)
                elif kind == "qk":
                    g, h, t = key
                    if (g, h, t) == ("a", 0, 1):
                        wait_cached("a")
                        pe.wait_ge(proj_taken, 2 * 12)
                    if (g, h, t) == ("c", 0, 0):
                        wait_cached("c")
                        pe.wait_ge(proj_taken, 2 * N_IN)
                    for m in range(1 if g == "a" else 2):
                        k = key + (m,)
                        pe.wait_ge(padded, pad_no[k] + 1)
                        qk.wait_free(pe, k)
                        b = qk.bank(k)
                        key_products(score_bank[b], pad_slot(key, m)[:, 0:tokens(t)[1]], feat(SLOT["k" + g] + h // 2),
                                     cache_t[:, cache_slot(g), h // 2, :], t).then_inc(qk_full[b], 1)
                elif kind == "pt":
                    g, h, t = key
                    rows, n, u = tokens(t)[1], keys(t), unit_no[key]
                    pe.wait_ge(p_ready, u + 1)
                    tr.wait_free(pe, step)
                    b = tr.bank(step)
                    for j in range((n + P - 1) // P):
                        w = min(P, n - P * j)
                        ins = nc.tensor.transpose(tr_bank[b][0:w, rows * j:rows * j + rows],
                                                  p_work[0:rows, 2 * (u % 3), P * j:P * j + w], ident[0:rows, 0:rows])
                    ins.then_inc(tr_full[b], 1)
                elif kind == "pv":
                    g, h, t = key
                    rows, n, u = tokens(t)[1], keys(t), unit_no[key]
                    if (g, h, t) == ("a", 0, 1):
                        pe.wait_ge(v_cache_in, 16)
                        wait_rows("va")
                    if (g, h, t) == ("c", 0, 0):
                        pe.wait_ge(v_cache_in, 48)
                        wait_rows("vc")
                    tr.wait_taken(pe, ("pt",) + key)
                    if o_uses[step]:
                        pe.wait_ge(o_free, o_uses[step])
                    r = slice(HD * (h % 2), HD * (h % 2) + HD)
                    nb = (n + P - 1) // P
                    for j in range(nb):
                        w = min(P, n - P * j)
                        kt = j if t < 4 else (4 + j)
                        ins = mm(o_bank[r, 0:rows], v_of(g)[0:w, kt, HD * h:HD * h + HD], p_t[0:w, u % 2, j, 0:rows],
                                 start=(j == 0), stop=(j == nb - 1))
                    ins.then_inc(o_full, 1)
                elif kind == "means":
                    pe.wait_ge(c_squared, key[0] + 1)
                    if key[0]:
                        pe.wait_ge(log_ready, 2 + key[0])
                    else:
                        pe.wait_ge(proj_taken, 2 * N_IN)
                    mm(bank[0][:, 0:N_PROMPT], two_heads[:, :], c_sq[:, 0:N_PROMPT], start=True, stop=True)\
                        .then_inc(means_full, 1)
                    tr.wait_free(pe, step)
                    mm(tr_bank[tr.bank(step)][:, 0:N_SAMPLE], two_heads[:, :], c_sq[:, N_PROMPT:NT], start=True, stop=True)\
                        .then_inc(tr_full[tr.bank(step)], 1)
                elif kind == "z":
                    g, h, j = key
                    if (g, h, j) == ("b", 0, 3):
                        wait_cached("b")
                        pe.wait_ge(proj_taken, 2 * N_IN)
                    qk.wait_free(pe, key)
                    b = qk.bank(key)
                    w = stick_width(key)
                    if g == "b":
                        pe.wait_ge(padded, pad_no[key + (0,)] + 1)
                        ins = mm(score_bank[b][:, 0:w], pad_slot(key, 0), feat(SLOT["qb"] + h // 2)[:, P * j:N_PROMPT],
                                 start=True, stop=True)
                    else:
                        rows = stick_rows(key)
                        r = slice(HD * h, HD * h + HD)
                        for i in range(H_B // 2):
                            k_s = (feat(SLOT["kb"] + i)[r, N_PROMPT:NT] if j == 2
                                   else cache_t[r, cache_slot("b"), i, P * j:P * j + P])
                            ins = mm(score_bank[b][0:rows, HD * i:HD * i + HD], k_s,
                                     feat(SLOT["qb"] + i)[r, N_PROMPT:NT], start=(i == 0), stop=(i == H_B // 2 - 1),
                                     skip_group_check=True)
                    ins.then_inc(qk_full[b], 1)
                elif kind == "acc":
                    g, h, j = key
                    u, b = stick_no[key], qk.bank(key)
                    rows, w = stick_rows(key), stick_width(key)
                    pe.wait_ge(sp_ready, u + 1)
                    out = score_bank[b]
                    add = dict(start=False, skip_group_check=True)
                    mm(out[0:rows, 0:w], neg_tri[0:rows, 0:rows], softplus(key)[0:rows, :], stop=False, **add)
                    if g == "b":
                        if j == 2:
                            mm(out[:, P:w], neg_ones[:, :], softplus(stick_key[u - 1])[:, 0:w - P], stop=False, **add)
                        elif j < 2:
                            pe.wait_ge(run_ready, 2 * h + 2 - j)
                            mm(out[:, P:w], neg_ones[:, :], run[:, j, 0:w - P], stop=False, **add)
                        ins = mm(out[:, 0:P], ident[:, :], diag_neg[:, :], stop=True, **add)
                    else:
                        for back in range(1, 3 - j):
                            later = N_SAMPLE if j + back == 2 else P
                            ins = mm(out[0:rows, 0:w], neg_ones[0:later, 0:rows], softplus(stick_key[u - back])[0:later, :],
                                     stop=(j + back == 2), **add)
                        if j == 2:
                            ins = mm(out[0:rows, 0:w], ident[0:rows, 0:rows],
                                     diag_neg_s[:, :, :].rearrange("p h q -> p (h q)"), stop=True, **add)
                    ins.then_inc(qk_full[b], 1)
                elif kind == "av":
                    g, h, j = key
                    u = stick_no[key]
                    rows, w = stick_rows(key), stick_width(key)
                    qk.wait_taken(pe, key)
                    if (g, h, j) == ("b", 0, 3):
                        pe.wait_ge(v_cache_in, 32)
                        wait_rows("vb")
                    if (g == "b" and j == 3) or (g == "s" and j == 2):
                        use = o_uses[("av", g, h, 0)]
                        if use:
                            pe.wait_ge(o_free, use)
                    if g == "b":
                        r = slice(HD * (h % 2), HD * (h % 2) + HD)
                        ins = mm(o_bank[r, P * j:N_PROMPT], v_of(g)[:, j, HD * h:HD * h + HD], a_t[:, u % 2, 0:w],
                                 start=(j == 3), stop=(j == 0), skip_group_check=True)
                    else:
                        r = slice(HD * h, HD * h + HD)
                        for i in range(H_B // 2):
                            hh = 2 * i + h
                            ins = mm(o_bank[r, HD * i:HD * i + HD],
                                     v_of(g)[0:rows, 4 + j, HD * hh:HD * hh + HD], a_t[0:rows, u % 2, HD * i:HD * i + HD],
                                     start=(j == 2 and i == 0), stop=(j == 0 and i == H_B // 2 - 1),
                                     skip_group_check=True)
                    ins.then_inc(av_done, 1)

            for n in range(N_IN, N_SPLIT):
                project(n)

            pe.wait_ge(resid_ready, 2 * KD)
            mean_square(1)

            def gate_up(n, slot, after):
                pe.wait_ge(gu_lo_ready, n + 1)
                for m in range(2):
                    for b in range(2):
                        if after:
                            pe.wait_ge(sg_ready if m == 0 else hid_ready, n * 2 + (b - 1))
                        for k in range(KD):
                            ins = three(bank[2 * m + b][:, 0:HALF], gu_hi[:, slot, m, k, :], gu_lo[:, slot, m, k, :],
                                        h_hi[:, k, halves(b)], h_lo[:, k, halves(b)], k == 0, k == KD - 1)
                        ins.then_inc(au_full, 1)

            def down(q, n_e, hid_before):
                for d in range(KD):
                    pe.wait_ge(d_lo_ready, q * KD + d + 1)
                    for b in range(2):
                        i = 2 * d + b
                        if not (isinstance(q, int) and q == 0 and i < 4):
                            pe.wait_ge(y_added, q * 2 * KD + (i - 3))
                        for e in range(n_e):
                            if d == 0:
                                pe.wait_ge(hid_lo_ready, hid_before + (2 * e + b + 1))
                            ins = three(bank[4 + i % 4][:, 0:HALF], d_hi[:, d % 2, e, :], d_lo[:, d % 2, e, :],
                                        hid_hi[:, e, halves(b)], hid_lo[:, e, halves(b)], e == 0, e == n_e - 1)
                        ins.then_inc(down_full, 1)

            pe.wait_ge(log_ready, 7)
            pe.wait_ge(gu_lo_ready, 1)
            for k in range(KD):
                pe.wait_ge(h_lo_ready, 2 * KD + k + 1)
                for m in range(2):
                    for b in range(2):
                        ins = three(bank[2 * m + b][:, 0:HALF], gu_hi[:, 0, m, k, :], gu_lo[:, 0, m, k, :],
                                    h_hi[:, k, halves(b)], h_lo[:, k, halves(b)], k == 0, k == KD - 1)
                        if k == KD - 1:
                            ins.then_inc(au_full, 1)
            pe.wait_ge(r_taken, 2)
            for b in range(2):
                for k in range(KD):
                    mm(bank[4 + b][:, 0:HALF], r_hl[:, k, :], h_hi[:, k, halves(b)], start=(k == 0), stop=False)
                    ins = mm(bank[4 + b][:, 0:HALF], r_hl[:, k, :], h_lo[:, k, halves(b)], start=False, stop=(k == KD - 1))
                ins.then_inc(r_full, 1)
            pe.wait_ge(r_taken, 5)
            for t in range(5):
                c0 = P * t if t < 4 else NT - P
                ins = mm(bank[7][:, N_EXPERTS * t:N_EXPERTS * t + N_EXPERTS], r_turned[:, c0:c0 + P], two_idents[:, :],
                         start=True, stop=True)
            ins.then_inc(r_full, 1)
            pe.wait_ge(r_taken, 6)
            down(0, 1, 0)
            pe.wait_ge(y_added, 2 * KD)
            for t in range(5):
                c0 = P * t if t < 4 else NT - P
                pe.wait_ge(gates_ready, t + 1)
                if t >= 2:
                    pe.wait_ge(gates_copied, t - 1)
                nc.tensor.transpose(bank[4 + t % 2][0:N_EXPERTS, 0:P], r_rows[:, t, 2, :], ident[:, :]).then_inc(gates_turned, 1)
            pe.wait_ge(gated, 2 * GROUP)

            def group(g):
                for e in range(GROUP):
                    gate_up(g * GROUP + (1 + e), (1 + e) % 2, True)
                down(g + 1, GROUP, g * 2 * GROUP + 2)

            with pe.Fori(0, N_GROUPS) as g:
                group(g)

            for i, (t, c) in enumerate(Y_PARTS):
                if i == 4:
                    pe.wait_ge(sq_used, 3 * KD)
                    for u in range(5):
                        c0, n = tokens(u)
                        ins = mm(bank[4][0:n, u:u + 1], rstd[:, c0:c0 + n], ones[:, 0:1], start=True, stop=True)
                    ins.then_inc(means_full, 1)
                c0, n = tokens(t)
                if i >= 7:
                    wait_y_taken(pe, i - 7)
                for j in range(4):
                    k = 4 * c + j
                    pe.wait_ge(scaled, k + 1)
                    ins = nc.tensor.transpose(Y_BANKS[i % 7][0:n, P * j:P * j + P], y_acc[:, k, c0:c0 + n], ident[:, :])
                ins.then_inc(y_full, 1)

        @block.vector
        def _(dve):
            v = nc.vector
            n_step = 0

            def chain(ins):
                nonlocal n_step
                n_step += 1
                ins.then_inc(dve_step, 1)
                dve.wait_ge(dve_step, n_step)

            def copy_modulation(n):
                dve.wait_ge(ada_rows, 4 * n + 4)
                if n:
                    dve.wait_ge(ada_full, n)
                v.tensor_copy(mod_rows[:, :], tr_bank[tr.bank(("ada", n))][0:2, :]).then_inc(rows_copied, 1)

            def modulation(n):
                step = ("ada", n)
                dve.wait_ge(ada_full, n + 1)
                part = tr_bank[tr.bank(step)][:, 0:8].rearrange("p (e b) -> p e b", b=2)
                add1 = 1.0 if n in (2, 3, 8, 9) else 0.0
                for b in range(2):
                    ins = v.scalar_tensor_tensor(out=mod[:, 4 * n:4 * n + 4, b], in0=part[:, :, b], scalar=add1,
                                                 in1=vec[:, 4 * n:4 * n + 4], op0=ALU.add, op1=ALU.add)
                tr.take(ins, step)

            def normed(src, dst, inc, tiles=range(KD + 1)):
                for k in tiles:
                    if k < KD:
                        if k >= 2:
                            dve.wait_ge(h_lo_ready, inc + k - 1)
                        v.tensor_tensor(dst[:, k % 2, :], src[:, k, :], rstd[:, :], ALU.mult).then_inc(norm_ready, 1)
                    if k:
                        low(dst[:, (k - 1) % 2, :], k - 1, inc)

            def low(src, k, base):
                dve.wait_ge(h_hi_ready, base + k + 1)
                v.tensor_tensor(h_lo[:, k, :], src, h_hi[:, k, :].bitcast(F32), ALU.subtract).then_inc(h_lo_ready, 1)

            def sum_square(r, k, buf):
                if k == 0:
                    return
                m = KD * r + k
                dve.wait_ge(sq_ready, m + 1)
                if k > 1:
                    dve.wait_ge(sq_used, m)
                ins = v.tensor_tensor(rstd[:, :], buf[:, 0, :] if k == 1 else rstd[:, :], buf[:, k % 2, :], ALU.add)
                ins.then_inc(sq_used, 2 if k == 1 else 1)

            dve.wait_ge(vec_turned, 1)
            v.tensor_copy(vec[:, :], bank[7][:, 0:73]).then_inc(vec_ready, 1)

            for kind, t in PROLOGUE:
                if kind == "ada":
                    copy_modulation(t)
                if kind == "turn":
                    modulation(t)
                if kind == "sum":
                    for k in range(KD):
                        sum_square(0, k, sq)
                if kind == "norm":
                    if t == 0:
                        dve.wait_ge(rstd_ready, 1)
                    else:
                        split_low(dve, v, 0)
                    normed(o_t, hf, 0, range(t, 4 if t == 0 else KD + 1))
                if kind != "x":
                    continue
                c0, n = tokens(t)
                for c in range(2):
                    m = 2 * t + c
                    dve.wait_ge(xt_full, m + 1)
                    v.tensor_copy(o_t[:, 4 * c:4 * c + 4, c0:c0 + n],
                                  bank[2 + m % 3][:, 0:4 * n].rearrange("p (k t) -> p k t", k=4)).then_inc(xt_taken, 1)
            dve.wait_ge(consts, N_CONSTS)
            chain(v.scalar_tensor_tensor(out=dist[:, :], in0=dist[:, :], scalar=-1.0, in1=dist[:, :], op0=ALU.mult,
                                         op1=ALU.max))
            chain(v.memset(dist[0:CHUNK, 512 - CHUNK:512], -NEG))
            chain(v.tensor_scalar(vec[:, 72:73], vec[:, 72:73], 1.0 - LAM_INIT, None, ALU.mult))
            dve.wait_ge(lam_in, 16)
            for i in range(2):
                a = lam_rows[:, 2 * QK_C * i:2 * QK_C * i + QK_C]
                b = lam_rows[:, 2 * QK_C * i + QK_C:2 * QK_C * (i + 1)]
                v.tensor_tensor_reduce(out=a, in0=a, in1=b, scale=1.0, scalar=0.0, op0=ALU.mult, op1=ALU.add,
                                       accum_out=lam_dot[:, i:i + 1]).then_inc(lam_dots, 1)
            dve.wait_ge(lam_exps, 1)
            chain(v.tensor_tensor(lam[:, :], lam_exp[:, 0:1], lam_exp[:, 1:2], ALU.subtract))
            chain(v.tensor_scalar(lam[:, :], lam[:, :], LAM_INIT, None, ALU.add))

            for step in SCHEDULE:
                kind, key = step[0], step[1:]

                if kind == "ada":
                    copy_modulation(step[1])
                elif kind == "turn":
                    modulation(step[1])
                elif kind == "score":
                    t, h = key
                    n, m, rows = keys(t), score_no[step], tokens(t)[1]
                    if m == 0:
                        for half in range(2):
                            tr.wait_taken(dve, ("rows", 1, half))
                    qk.wait_taken(dve, step)
                    rel, w, out = bias[0:rows, m % 2, 0:n], wi_rows[0:rows, t, h:h + 1], pick[t][0:rows, :]
                    if h == 0:
                        v.tensor_scalar(out, rel, w, None, ALU.mult).then_inc(score_ready, 1)
                    else:
                        dve.wait_ge(score_ready, m)
                        v.scalar_tensor_tensor(out=out, in0=rel, scalar=w, in1=out, op0=ALU.mult, op1=ALU.add)\
                            .then_inc(score_ready, 1)
                elif kind == "topk":
                    t = step[1]
                    rows, n = tokens(t)[1], keys(t)
                    s = pick[t][0:rows, :]
                    dve.wait_ge(score_ready, score_no[("score", t, N_IDX - 1)] + 1)
                    if t < 4:
                        chain(v.memset(pick[t][0:CHUNK, n - CHUNK:n], INVALID))
                    for _ in range((TOPK_PROMPT if t < 4 else TOPK_SAMPLE) // 8):
                        chain(v.max(max8[0:rows, :], s))
                        chain(v.match_replace(s, max8[0:rows, :], s, CHOSEN))
                    v.tensor_scalar(s, s, (CHOSEN + INVALID) / 2, NEG, ALU.is_gt, ALU.mult).then_inc(picked, 1)
                elif kind == "max":
                    g, h, t = key
                    rows, n, u = tokens(t)[1], keys(t), unit_no[key]
                    d0 = DIST0 - P * t if t < 4 else DIST0 - PAST
                    if g == "a":
                        slot, scale = u % 2, SCALE_A
                        tab = bias[0:rows, slot, 0:n]
                        dr = dist[0:rows, d0:d0 + n]
                        if u >= 2:
                            qk.wait_taken(dve, unit_key[u - 2] + (0,))
                        if t:
                            dve.wait_ge(picked, t)
                            chain(v.scalar_tensor_tensor(out=tab, in0=dr, scalar=-SLOPE_A[h] / SCALE_A,
                                                         in1=pick[t][0:rows, :], op0=ALU.mult, op1=ALU.add))
                        else:
                            chain(v.tensor_scalar(tab, dr, -SLOPE_A[h] / SCALE_A, None, ALU.mult))
                    else:
                        slot, scale = h % 2, SCALE_C
                        dve.wait_ge(bias_ready, h + 1)
                        tab = bias[0:rows, slot, d0:d0 + n]
                    if u >= 3:
                        tr.wait_full(dve, ("pt",) + unit_key[u - 3])
                        dve.wait_ge(p_ready, u - 2)
                    for m in range(2 if g == "c" else 1):
                        k = key + (m,)
                        qk.wait_full(dve, k)
                        qk.take(v.tensor_tensor_reduce(out=p_work[0:rows, 2 * (u % 3) + m, 0:n],
                                                       in0=score_bank[qk.bank(k)][0:rows, 0:n], in1=tab,
                                                       scale=-scale, scalar=3e38, op0=ALU.add, op1=ALU.min,
                                                       accum_out=n_max[0:rows, u % 2, m:m + 1]), k)
                elif kind == "norm":
                    g, h, t = key
                    rows, n, u = tokens(t)[1], keys(t), unit_no[key]
                    maps = 2 if g == "c" else 1
                    dve.wait_ge(exp_ready, map_no[key + (maps - 1,)] + 1)
                    e = [p_work[0:rows, 2 * (u % 3) + m, 0:n] for m in range(2)]
                    rec = p_rec[0:rows, u % 2, :]
                    if u >= 2:
                        dve.wait_ge(p_ready, u - 1)
                    chain(v.reciprocal(rec[:, 0:maps], p_sum[0:rows, u % 2, 0:maps]))
                    if g == "a":
                        v.tensor_scalar(e[0], e[0], rec[:, 0:1], None, ALU.mult).then_inc(p_ready, 1)
                    else:
                        chain(v.tensor_scalar(e[1], e[1], rec[:, 1:2], lam[0:rows, :], ALU.mult, ALU.mult))
                        v.scalar_tensor_tensor(out=e[0], in0=e[0], scalar=rec[:, 0:1], in1=e[1], op0=ALU.mult,
                                               op1=ALU.subtract).then_inc(p_ready, 1)
                elif kind == "pv" and key[0] == "a":
                    g, h, t = key
                    c0, rows = tokens(t)
                    if unit_no[key] == 0:
                        dve.wait_ge(spilled, 16)
                    r = slice(HD * (h % 2), HD * (h % 2) + HD)
                    dve.wait_ge(o_full, unit_no[key] + 1)
                    v.tensor_copy(o_t[r, MIX[g] + h // 2, c0:c0 + rows], o_bank[r, 0:rows]).then_inc(o_free, 1)
                elif kind == "root":
                    i = key[0]
                    o = o_t[:, MIX["c"] + i, :]
                    dve.wait_ge(rstd_ready, 2 + i)
                    v.scalar_tensor_tensor(out=o, in0=o, scalar=vec[:, 72:73], in1=rstd[:, :], op0=ALU.mult,
                                           op1=ALU.mult).then_inc(c_normed, 1)
                elif kind == "split_o" and key[0] >= MIX["c"]:
                    k = key[0]
                    if k == MIX["c"]:
                        dve.wait_ge(h_lo_ready, KD + MIX["c"])
                    low(o_t[:, k, :], k, KD)
                elif kind == "z":
                    rows, w, u = stick_rows(key), stick_width(key), stick_no[key]
                    qk.wait_full(dve, key, 1)
                    if u == 0:
                        dve.wait_ge(o_full, unit_no[last_a_pv[1:]] + 1)
                    if u >= 2:
                        dve.wait_ge(sp_ready, u - 1)
                    v.tensor_scalar(l_buf[0:rows, u % 2, 0:w], score_bank[qk.bank(key)][0:rows, 0:w], BIG_Z, None,
                                    ALU.min).then_inc(capped, 1)
                elif kind == "sp":
                    g, h, j = key
                    rows, w, u = stick_rows(key), stick_width(key), stick_no[key]
                    dve.wait_ge(l_ready, u + 1)
                    if u >= 3:
                        by_next = stick_key[u - 2][0] == "b" and stick_key[u - 2][2] == 2
                        qk.wait_full(dve, stick_key[u - (2 if by_next else 3)], 2)
                    sums = len([k for k in list(stick_no)[:max(u - 1, 0)] if k[0] == "b" and k[2] in (1, 2)])
                    if sums:
                        dve.wait_ge(run_ready, sums)
                    sp = softplus(key)[0:rows, :]
                    ins = v.tensor_tensor(sp[:, 0:w], score_bank[qk.bank(key)][0:rows, 0:w], l_buf[0:rows, u % 2, 0:w],
                                          ALU.max)
                    if g == "b":
                        chain(ins)
                        ins = v.tensor_tensor(sp[:, 0:P], sp[:, 0:P], diag_01[:, :], ALU.mult)
                    elif j == 2:
                        chain(ins)
                        ins = v.tensor_tensor(sp[:, 0:w], sp[:, 0:w], diag_01_s[:, :, :].rearrange("p h q -> p (h q)"),
                                              ALU.mult)
                    ins.then_inc(sp_ready, 1)
                    if g == "b" and j in (1, 2):
                        dve.wait_ge(sp_ready, u + 1)
                        later = softplus(stick_key[u - 1])[:, 0:P] if j == 2 else run[:, 1, 0:2 * P]
                        if j == 1:
                            dve.wait_ge(run_ready, 2 * h + 1)
                        chain(v.tensor_copy(run[:, j - 1, 0:P], sp[:, 0:P]))
                        v.tensor_tensor(run[:, j - 1, P:w], sp[:, P:w], later, ALU.add).then_inc(run_ready, 1)
                elif kind == "av" and key[2] == 0:
                    g, h, j = key
                    dve.wait_ge(av_done, stick_no[key] + 1)
                    if g == "b":
                        r = slice(HD * (h % 2), HD * (h % 2) + HD)
                        dst, src = o_t[r, MIX["b"] + h // 2, 0:N_PROMPT], o_bank[r, 0:N_PROMPT]
                    else:
                        r = slice(HD * h, HD * h + HD)
                        dst = o_t[r, MIX["b"]:MIX["c"], N_PROMPT:NT]
                        src = o_bank[r, 0:3 * N_SAMPLE].rearrange("p (i q) -> p i q", i=3)
                    v.tensor_copy(dst, src).then_inc(o_free, 1)

            def gu_low(n, s):
                dve.wait_ge(gu_hi_ready, n + 1)
                v.tensor_tensor(gu_lo[:, s], gu_stage[:, s], gu_hi[:, s].bitcast(F32), ALU.subtract)\
                    .then_inc(gu_lo_ready, 1)

            dve.wait_ge(resid_in, 16)
            for n in range(4, 12):
                tr.wait_taken(dve, ("ada", n))
            for e in range(KD):
                n = N_IN + e
                if e == 1:
                    dve.wait_ge(w_lo_ready, n + 1)
                if 0 < e < KD - 1:
                    split_low(dve, v, n + 1)
                if e == KD - 1:
                    gu_low(0, 0)
                for b in range(2):
                    dve.wait_ge(proj_full, 2 * n + b + 1)
                    parts = [(0, HALF, 0)] if b == 0 else [(HALF, N_PROMPT, 0), (N_PROMPT, NT, 1)]
                    for a, z, stream in parts:
                        r = resid[:, e, a:z]
                        ins = v.scalar_tensor_tensor(out=r, in0=bank[b][:, a - HALF * b:z - HALF * b],
                                                     scalar=mod[:, 2 * KD + e, stream:stream + 1], in1=r,
                                                     op0=ALU.mult, op1=ALU.add)
                    ins.then_inc(resid_ready, 1)
                if e:
                    sum_square(1, e - 1, sq)
            sum_square(1, KD - 1, sq)

            def down_low(n_d, d, n_e):
                dve.wait_ge(d_hi_ready, n_d + 1)
                v.tensor_tensor(d_lo[:, d % 2, 0:n_e, :], d_stage[:, 0:n_e, P * d:P * d + P],
                                d_hi[:, d % 2, 0:n_e, :].bitcast(F32), ALU.subtract).then_inc(d_lo_ready, 1)

            def hidden(n, slot, e, routed):
                hv = [slice(HALF * b, HALF * b + HALF) for b in range(2)]
                if routed:
                    g = routed[0]
                    dve.wait_ge(g_in[e], g * 16 + 16)
                    for b in range(2):
                        dve.wait_ge(sg_ready, n * 2 + (b + 1))
                        v.tensor_tensor(sg[:, slot, hv[b]], sg[:, slot, hv[b]], gate_bc[:, e, hv[b]], ALU.mult)\
                            .then_inc(gated, 1)
                for b in range(2):
                    if routed:
                        dve.wait_ge(gated, n * 2 + (2 * GROUP - 2 + b + 1))
                    else:
                        dve.wait_ge(sg_ready, n * 2 + (b + 1))
                    dve.wait_ge(au_full, n * 4 + (2 + b + 1))
                    if routed:
                        dve.wait_ge(hid_lo_ready, n * 2)
                    v.tensor_tensor(hidf[:, slot, hv[b]], sg[:, slot, hv[b]], bank[2 + b][:, 0:HALF], ALU.mult)\
                        .then_inc(hid_ready, 1)
                for b in range(2):
                    dve.wait_ge(hid_hi_ready, n * 2 + (b + 1))
                    v.tensor_tensor(hid_lo[:, e, hv[b]], hidf[:, slot, hv[b]], hid_hi[:, e, hv[b]].bitcast(F32),
                                    ALU.subtract).then_inc(hid_lo_ready, 1)

            def add_y(q, d, first):
                for b in range(2):
                    i = 2 * d + b
                    dve.wait_ge(down_full, q * 2 * KD + (i + 1))
                    y, part = y_acc[:, d, HALF * b:HALF * b + HALF], bank[4 + i % 4][:, 0:HALF]
                    if first:
                        ins = v.tensor_copy(y, part)
                    else:
                        dve.wait_ge(y_added, q * 2 * KD + (i - 2 * KD + 1))
                        ins = v.tensor_tensor(y, part, y, ALU.add)
                    ins.then_inc(y_added, 1)

            dve.wait_ge(rstd_ready, 5)
            normed(resid, hidf, 2 * KD)
            dve.wait_ge(r_taken, 1)
            v.tensor_tensor(r_hl[:, :, N_EXPERTS:P], r_stage, r_hl[:, :, 0:N_EXPERTS].bitcast(F32), ALU.subtract)\
                .then_inc(r_taken, 1)
            v.tensor_tensor(two_idents[:, :], ident[:, 0:N_EXPERTS], ident[:, N_EXPERTS:P], ALU.add).then_inc(r_taken, 1)
            hidden(0, 0, 0, None)
            gu_low(1, 1)
            down_low(0, 0, 1)
            down_low(1, 1, 1)

            dve.wait_ge(r_taken, 6)
            part = [[r_rows[:, t, i, :] for t in range(5)] for i in range(3)]
            for t in range(5):
                ins = v.tensor_tensor(part[1][t], part[0][t], b_rows[:, :], ALU.add)
            chain(ins)
            for t in range(5):
                ins = v.max(r_max[:, t, :], part[1][t])
            chain(ins)
            for t in range(5):
                ins = v.match_replace(part[1][t], r_max[:, t, :], part[1][t], CHOSEN)
            chain(ins)
            for t in range(5):
                ins = v.scalar_tensor_tensor(out=part[2][t], in0=part[1][t], scalar=(CHOSEN + INVALID) / 2,
                                             in1=part[0][t], op0=ALU.is_lt, op1=ALU.mult, accum_out=r_sum[:, t, 0:1])
            chain(ins)
            chain(v.reciprocal(r_sum[:, :, 1], r_sum[:, :, 0]))
            for t in range(5):
                v.tensor_scalar(part[2][t], part[2][t], r_sum[:, t, 1:2], ROUTED_SCALE, ALU.mult, ALU.mult)\
                    .then_inc(gates_ready, 1)
            for d in range(KD):
                add_y(0, d, True)
                if d + 2 < KD:
                    down_low(d + 2, d + 2, 1)
            for t in range(5):
                c0 = P * t if t < 4 else NT - P
                dve.wait_ge(gates_turned, t + 1)
                if t == 4:
                    dve.wait_ge(gates_copied, 4)
                ins = v.tensor_copy(gate_t[:, c0:c0 + P], bank[4 + t % 2][0:N_EXPERTS, 0:P])
                if t < 4:
                    ins.then_inc(gates_copied, 1)
                else:
                    ins.then_inc(gated, 2 * GROUP)

            def last_residual(k):
                dve.wait_ge(y_added, (N_GROUPS * KD + k + 1) * 2)
                for b, (a, z) in enumerate(((0, N_PROMPT), (N_PROMPT, NT))):
                    r = resid[:, k, a:z]
                    ins = v.scalar_tensor_tensor(out=r, in0=y_acc[:, k, a:z], scalar=mod[:, 5 * KD + k, b:b + 1], in1=r,
                                                 op0=ALU.mult, op1=ALU.add)
                ins.then_inc(fin_ready, 1)

            def group(g, last):
                for e in range(GROUP):
                    n = g * GROUP + (1 + e)
                    if e < GROUP - 1:
                        gu_low(n + 1, (2 + e) % 2)
                    else:
                        down_low(g * KD + KD, 0, GROUP)
                        down_low(g * KD + (KD + 1), 1, GROUP)
                    hidden(n, (1 + e) % 2, e, (g,))
                for d in range(KD):
                    add_y(g + 1, d, False)
                    if d + 2 < KD:
                        down_low(g * KD + (KD + d + 2), d + 2, GROUP)
                    if d == 2 and not last:
                        gu_low(g * GROUP + (GROUP + 1), 1)
                    if last:
                        last_residual(d)
                        if d:
                            sum_square(2, d - 1, sg)

            with dve.Fori(0, N_GROUPS - 1) as g:
                group(g, False)
            group(N_GROUPS - 1, True)

            sum_square(2, KD - 1, sg)
            for i, (rows, t) in enumerate(((P, slice(0, 4)), (N_SAMPLE, slice(4, 5)))):
                dve.wait_ge(row_root_ready, i + 1)
                v.reciprocal(row_rstd[0:rows, t], row_root[0:rows, t]).then_inc(row_rstd_ready, 1)
            dve.wait_ge(row_rstd_ready, 2)
            for i in range(1, len(Y_PARTS), 2):
                rows, turned_y, inverse = y_part(i)
                dve.wait_ge(y_full, i + 1)
                v.tensor_scalar(rows, turned_y, inverse, None, ALU.mult).then_inc(y_taken[1], 1)


OUTPUTS = {
    "y_prompt": (1, N_PROMPT, D), "y_sample": (1, N_SAMPLE, D),
    "kv_a_p": (1, 1, N_PROMPT, 2, H_A, HD), "ki_p": (1, 1, N_PROMPT, HD),
    "kv_b_p": (1, 1, N_PROMPT, 2, H_B, HD), "kv_c_p": (1, 1, N_PROMPT, 2, H_C, HD),
    "kv_a_s": (1, 1, N_SAMPLE, 2, H_A, HD), "ki_s": (1, 1, N_SAMPLE, HD),
    "kv_b_s": (1, 1, N_SAMPLE, 2, H_B, HD), "kv_c_s": (1, 1, N_SAMPLE, 2, H_C, HD),
}


def kernel(**inputs):
    import numpy as np
    import concourse.bacc as bacc
    from concourse.bass_utils import run_bass_kernel_spmd

    nc = bacc.Bacc("TRN2", target_bir_lowering=False, num_devices=1)
    io, arrays = {}, {}
    for name, value in inputs.items():
        a = np.ascontiguousarray(value)
        arrays[f"in_{name}"] = a
        io[name] = nc.dram_tensor(f"in_{name}", a.shape, mybir.dt.from_np(a.dtype), kind="ExternalInput").ap()
    for name, shape in OUTPUTS.items():
        ap = nc.dram_tensor(f"out_{name}", shape, F32, kind="ExternalOutput").ap()
        if name.startswith("kv"):
            ap = ap[0, 0].rearrange("t kv h d -> t kv (h d)")
        elif name.startswith("ki"):
            ap = ap[0, 0]
        io[name] = ap
    build(nc, io)
    r = run_bass_kernel_spmd(nc, [arrays], core_ids=[0])
    return tuple(r.results[0][f"out_{name}"] for name in OUTPUTS)
```
